# Optimizing a Trainium2 kernel written in Bass

```python
import jax, jax.numpy as jnp
from jax import lax
import numpy as np

D_MODEL = 1024
BATCH = 1
SEQ = 256
DEPTH = 2

N_MIXERS = 2
N_A_LAYERS = (DEPTH + 1) // 2
N_B_LAYERS = DEPTH // 2
NORM_EPS = 1e-6

A_WIDTH = 2 * D_MODEL
A_GROUPS = 8
A_CHUNK = 128
A_GROUP_DIM = A_WIDTH // A_GROUPS

B_HEADS = 4
B_KEY_DIM = D_MODEL // 2
B_VAL_DIM = D_MODEL
B_HEAD_K = B_KEY_DIM // B_HEADS
B_HEAD_V = B_VAL_DIM // B_HEADS
B_GATE_RANK = 16
B_GATE_NORM = 16.0
B_CHUNK = 64
B_PROJ = 2 * B_KEY_DIM + 2 * B_VAL_DIM + B_GATE_RANK

P_HEADS = 8
P_NKEYS = 128
P_EXPERTS = P_NKEYS * P_NKEYS
P_QDIM = 256
P_HALF = P_QDIM // 2
P_TOPK = 16
P_BLOCK = 128

kernel_name = "hybrid_gmlp_gla_peer_trunk"

def rmsnorm(x, g):
    xf = x.astype(jnp.float32)
    y = xf * lax.rsqrt(jnp.mean(xf * xf, axis=-1, keepdims=True) + NORM_EPS)
    return (y * g.astype(jnp.float32)).astype(x.dtype)

def layernorm(x, g, b):
    xf = x.astype(jnp.float32)
    mu = jnp.mean(xf, axis=-1, keepdims=True)
    xc = xf - mu
    y = xc * lax.rsqrt(jnp.mean(xc * xc, axis=-1, keepdims=True) + NORM_EPS)
    return (y * g.astype(jnp.float32) + b.astype(jnp.float32)).astype(x.dtype)

def mixer_a(h, w_in, b_in, ln_g, ln_b, w_s, b_s, w_out):
    B, L, _ = h.shape
    z = jax.nn.gelu(h @ w_in + b_in, approximate=False)
    u, v = jnp.split(z, 2, axis=-1)
    v = layernorm(v, ln_g, ln_b)
    v = v.reshape(B, L // A_CHUNK, A_CHUNK, A_GROUPS, A_GROUP_DIM)
    causal = jnp.tril(jnp.ones((A_CHUNK, A_CHUNK), dtype=bool))
    w = jnp.where(causal[None], w_s, 0.0)
    sv = jnp.einsum('gts,bnsgc->bntgc', w, v) + b_s.T[:, :, None]
    y = u * sv.reshape(B, L, A_WIDTH)
    return y @ w_out

def mixer_b(h, w_in, w_g2, b_g, norm_g, w_out):
    B, L, _ = h.shape
    f32 = jnp.float32
    proj = h @ w_in
    q, k, v, r, g_lr = jnp.split(
        proj, [B_KEY_DIM, 2 * B_KEY_DIM, 2 * B_KEY_DIM + B_VAL_DIM, 2 * B_KEY_DIM + 2 * B_VAL_DIM], axis=-1)
    log_a = jax.nn.log_sigmoid((g_lr @ w_g2 + b_g).astype(f32)) / B_GATE_NORM
    nc = L // B_CHUNK

    def to_chunks(t, d):
        return t.astype(f32).reshape(B, nc, B_CHUNK, B_HEADS, d).transpose(1, 0, 3, 2, 4)

    qc = to_chunks(q, B_HEAD_K) * (B_HEAD_K ** -0.5)
    kc = to_chunks(k, B_HEAD_K)
    vc = to_chunks(v, B_HEAD_V)
    gc = jnp.cumsum(to_chunks(log_a, B_HEAD_K), axis=3)
    causal = jnp.tril(jnp.ones((B_CHUNK, B_CHUNK), dtype=bool))[:, :, None]

    def step(S, inp):
        qb, kb, vb, gb = inp
        diff = gb[:, :, :, None, :] - gb[:, :, None, :, :]
        decay = jnp.where(causal, jnp.exp(jnp.where(causal, diff, 0.0)), 0.0)
        scores = jnp.einsum('bhtsk,bhsk->bhts', qb[:, :, :, None, :] * decay, kb)
        o = scores @ vb + jnp.einsum('bhtk,bhkv->bhtv', qb * jnp.exp(gb), S)
        g_last = gb[:, :, -1:, :]
        S = jnp.exp(g_last[:, :, 0, :, None]) * S + jnp.einsum(
            'bhsk,bhsv->bhkv', kb * jnp.exp(g_last - gb), vb)
        return S, o

    S0 = jnp.zeros((B, B_HEADS, B_HEAD_K, B_HEAD_V), f32)
    _, o = lax.scan(step, S0, (qc, kc, vc, gc))
    o = o.transpose(1, 0, 3, 2, 4).reshape(B, L, B_HEADS, B_HEAD_V)
    o = rmsnorm(o, norm_g).reshape(B, L, B_VAL_DIM).astype(h.dtype)
    o = o * jax.nn.silu(r)
    return o @ w_out

def peer(h, w_q, k1, k2, u_tab, v_tab):
    B, L, D = h.shape
    f32 = jnp.float32
    xs = h.reshape(-1, P_BLOCK, D)

    def block(xb):
        q = (xb @ w_q).reshape(P_BLOCK, P_HEADS, P_QDIM).astype(f32)
        s1 = jnp.einsum('thd,nd->thn', q[..., :P_HALF], k1.astype(f32))
        s2 = jnp.einsum('thd,nd->thn', q[..., P_HALF:], k2.astype(f32))
        v1, i1 = lax.top_k(s1, P_TOPK)
        v2, i2 = lax.top_k(s2, P_TOPK)
        cand = (v1[..., :, None] + v2[..., None, :]).reshape(P_BLOCK, P_HEADS, P_TOPK * P_TOPK)
        cand_id = (i1[..., :, None] * P_NKEYS + i2[..., None, :]).reshape(P_BLOCK, P_HEADS, P_TOPK * P_TOPK)
        top_s, pos = lax.top_k(cand, P_TOPK)
        eid = jnp.take_along_axis(cand_id, pos, axis=-1)
        gate = jax.nn.softmax(top_s, axis=-1)
        u_e = jnp.take(u_tab, eid, axis=0)
        act = jax.nn.gelu(jnp.einsum('thkd,td->thk', u_e, xb), approximate=False)
        v_e = jnp.take(v_tab, eid, axis=0)
        return jnp.einsum('thk,thkd->td', (gate * act).astype(xb.dtype), v_e)

    return lax.map(block, xs).reshape(B, L, D)

def setup_inputs(seed: int = 0) -> dict:
    key = jax.random.key(seed)
    ks = jax.random.split(key, 24)
    f32 = jnp.float32

    def nrm(k, shape, scale):
        return jax.random.normal(k, shape, f32) * scale

    return {
        "x": nrm(ks[0], (BATCH, SEQ, D_MODEL), 1.0),
        "norm_mix": 1.0 + nrm(ks[1], (DEPTH, D_MODEL), 0.02),
        "norm_ffn": 1.0 + nrm(ks[2], (DEPTH, D_MODEL), 0.02),
        "final_norm": 1.0 + nrm(ks[3], (D_MODEL,), 0.02),
        "a_w_in": nrm(ks[4], (N_A_LAYERS, D_MODEL, 2 * A_WIDTH), D_MODEL ** -0.5),
        "a_b_in": nrm(ks[5], (N_A_LAYERS, 2 * A_WIDTH), 0.02),
        "a_ln_g": 1.0 + nrm(ks[6], (N_A_LAYERS, A_WIDTH), 0.02),
        "a_ln_b": nrm(ks[7], (N_A_LAYERS, A_WIDTH), 0.02),
        "a_w_s": nrm(ks[8], (N_A_LAYERS, A_GROUPS, A_CHUNK, A_CHUNK), A_CHUNK ** -0.5),
        "a_b_s": 1.0 + nrm(ks[9], (N_A_LAYERS, A_GROUPS, A_CHUNK), 0.02),
        "a_w_out": nrm(ks[10], (N_A_LAYERS, A_WIDTH, D_MODEL), A_WIDTH ** -0.5),
        "b_w_in": nrm(ks[11], (N_B_LAYERS, D_MODEL, B_PROJ), D_MODEL ** -0.5),
        "b_w_g2": nrm(ks[12], (N_B_LAYERS, B_GATE_RANK, B_KEY_DIM), B_GATE_RANK ** -0.5),
        "b_b_g": nrm(ks[13], (N_B_LAYERS, B_KEY_DIM), 0.02),
        "b_norm": 1.0 + nrm(ks[14], (N_B_LAYERS, B_HEAD_V), 0.02),
        "b_w_out": nrm(ks[15], (N_B_LAYERS, B_VAL_DIM, D_MODEL), B_VAL_DIM ** -0.5),
        "p_w_q": nrm(ks[16], (DEPTH, D_MODEL, P_HEADS * P_QDIM), D_MODEL ** -0.5),
        "p_k1": nrm(ks[17], (DEPTH, P_NKEYS, P_HALF), P_HALF ** -0.5),
        "p_k2": nrm(ks[18], (DEPTH, P_NKEYS, P_HALF), P_HALF ** -0.5),
        "p_u": nrm(ks[19], (DEPTH, P_EXPERTS, D_MODEL), D_MODEL ** -0.5),
        "p_v": nrm(ks[20], (DEPTH, P_EXPERTS, D_MODEL), P_HEADS ** -0.5),
    }

def reference(x, norm_mix, norm_ffn, final_norm,
              a_w_in, a_b_in, a_ln_g, a_ln_b, a_w_s, a_b_s, a_w_out,
              b_w_in, b_w_g2, b_b_g, b_norm, b_w_out,
              p_w_q, p_k1, p_k2, p_u, p_v):
    for i in range(DEPTH):
        h = rmsnorm(x, norm_mix[i])
        j = i // N_MIXERS
        if i % N_MIXERS == 0:
            x = x + mixer_a(h, a_w_in[j], a_b_in[j], a_ln_g[j], a_ln_b[j], a_w_s[j], a_b_s[j], a_w_out[j])
        else:
            x = x + mixer_b(h, b_w_in[j], b_w_g2[j], b_b_g[j], b_norm[j], b_w_out[j])
        h = rmsnorm(x, norm_ffn[i])
        x = x + peer(h, p_w_q[i], p_k1[i], p_k2[i], p_u[i], p_v[i])
    return rmsnorm(x, final_norm)


_drawn_inputs = setup_inputs


def setup_inputs(seed=0):
    import zlib

    import numpy as np

    out = dict(_drawn_inputs(seed))
    spreads = {}
    factors = {'final_norm': 2.986, 'b_b_g': 6.669, 'b_norm': 3.887}
    for name, (base, spread) in spreads.items():
        noise = np.random.default_rng([zlib.crc32(name.encode()), seed]).standard_normal(out[name].shape)
        drawn = base * np.exp(spread * noise) if base else spread * noise
        out[name] = __import__('jax').numpy.asarray(drawn.astype(out[name].dtype))
    for name, factor in factors.items():
        out[name] = (out[name] * factor).astype(out[name].dtype)
    return out
```

```python
from contextlib import ExitStack

import numpy as np

import concourse.bass as bass
from concourse import mybir

F32 = mybir.dt.float32
F32R = mybir.dt.float32r
U32 = mybir.dt.uint32
ALU = mybir.AluOpType
ACT = mybir.ActivationFunctionType
AX = mybir.AxisListType

P = 128
D = 1024
KB = D // P
T = 256
TT = T // P
TILE = 1024
BANK = 512
EPS = 1e-6

A_WIDTH = 2048
A_GROUPS = 8
A_GDIM = A_WIDTH // A_GROUPS
A_BLOCKS = 2 * A_WIDTH // TILE
YB = A_WIDTH // P

B_HEADS = 4
B_HK = 128
B_HV = 256
B_KEY = B_HEADS * B_HK
B_RANK = 16
B_LEVELS = 7

P_HEADS = 8
P_ROWS = 2 * P_HEADS
NK = 128
TOPK = 16
PICKS = P_HEADS * TOPK

RAW_SLOTS = 4
SPLIT_SLOTS = 2
LOWEST = -3.0e38

N_AIN = A_BLOCKS * KB
N_AOUT = YB
N_WQ = P_ROWS
N_EXP = NK
N_BQK = 2 * B_KEY // P
N_BVR = 2 * KB
N_BOUT = KB
AIN = 0
AOUT = AIN + N_AIN
WQ = [AOUT + N_AOUT, 0]
UT = [WQ[0] + N_WQ, 0]
VT = [UT[0] + N_EXP, 0]
BQK = VT[0] + N_EXP
BVR = BQK + N_BQK
BOUT = BVR + N_BVR
WQ[1] = BOUT + N_BOUT
UT[1] = WQ[1] + N_WQ
VT[1] = UT[1] + N_EXP
TILES = VT[1] + N_EXP


def trunk(nc, t, out):
    with ExitStack() as ctx:
        def sb(name, shape, dt=F32):
            return ctx.enter_context(nc.sbuf_tensor(name, shape, dt))

        def sem(name):
            return ctx.enter_context(nc.semaphore(name))

        raw = [sb(f"raw{s}", [P, TILE]) for s in range(RAW_SLOTS)]
        tile_hi = [sb(f"tile_hi{s}", [P, TILE], F32R) for s in range(SPLIT_SLOTS)]
        tile_lo = [sb(f"tile_lo{s}", [P, TILE], F32R) for s in range(SPLIT_SLOTS)]
        hT_hi = sb("hT_hi", [P, KB, T], F32R)
        hT_lo = sb("hT_lo", [P, KB, T], F32R)
        x = sb("x", [P, TT, D])
        w_hi = [sb(f"w_hi{s}", [P, T], F32R) for s in range(SPLIT_SLOTS)]
        w_lo = [sb(f"w_lo{s}", [P, T], F32R) for s in range(SPLIT_SLOTS)]
        consts = sb("consts", [P, 3, P])
        ident, iota, tri16 = consts[:, 0, :], consts[:, 1, :], consts[:, 2, :]
        keysT = sb("keysT", [P, 2, 2, NK])
        gains = sb("gains", [P, 4, KB])
        b_sT = sb("b_sT", [P, A_GROUPS])
        picks = sb("picks", [P, TT, 3, PICKS])
        picksT = sb("picksT", [P, 3, T])
        sumsq = sb("sumsq", [P, TT])
        meansq = sb("meansq", [P, TT])
        rms = sb("rms", [P, TT])
        rstd = sb("rstd", [P, TT])
        v_sum = sb("v_sum", [P, TT, 2])
        v_mean = sb("v_mean", [P, TT])
        head_sum = sb("head_sum", [P, TT, P_HEADS])
        head_inv = sb("head_inv", [P, TT, P_HEADS])

        def overlay(parts):
            with ExitStack() as own:
                return [own.enter_context(nc.sbuf_tensor(*p)) for p in parts]

        onehot1, onehot2 = overlay([("onehot1", [P, 8, P], F32), ("onehot2", [P, 8, P], F32)])
        (topv, topi, topi_f, candv, candpos, pos_a, pos_b, pos_af, pos_bf) = overlay([
            ("topv", [P, TT, P_ROWS, TOPK], F32),
            ("topi", [P, TT, P_ROWS, TOPK], U32),
            ("topi_f", [P, P_ROWS, TOPK], F32),
            ("candv", [P, P_HEADS, TOPK], F32),
            ("candpos", [P, P_HEADS, TOPK], U32),
            ("pos_a", [P, P_HEADS, TOPK], U32),
            ("pos_b", [P, P_HEADS, TOPK], U32),
            ("pos_af", [P, P_HEADS, TOPK], F32),
            ("pos_bf", [P, P_HEADS, TOPK], F32),
        ])
        reserved_small = sb("reserved_small", [P, 2048])

        (acts,) = overlay([("acts", [P, NK, T], F32)])
        (_, qT, scores, cand, look) = overlay([
            ("pad_peer", [P, 80 * T], F32),
            ("qT", [P, P_ROWS, T], F32),
            ("scores", [P, TT, P_ROWS, NK], F32),
            ("cand", [P, P_HEADS, TOPK * TOPK], F32),
            ("look", [P, P_HEADS, TOPK, TOPK], F32),
        ])
        (b_in, ln_g, ln_b, zv, zu, wsT, yT_hi, yT_lo) = overlay([
            ("b_in", [P, 2 * A_WIDTH], F32),
            ("ln_g", [P, A_WIDTH], F32),
            ("ln_b", [P, A_WIDTH], F32),
            ("zv", [P, TT, A_WIDTH], F32),
            ("zu", [P, TT, A_WIDTH], F32),
            ("wsT", [P, A_GROUPS, P], F32),
            ("yT_hi", [P, YB, T], F32R),
            ("yT_lo", [P, YB, T], F32R),
        ])
        (gq, gk, gcum, z_la, z_tmp, ed0, ed1, qe0, qe1, ke0, ke1, score_in, score_x, bv, br, bsg, bo, bg_row,
         bnorm_row, w_g2, w_g, masks, g_lrT, head_ms) = overlay([
            ("gq", [P, B_HEADS, T], F32),
            ("gk", [P, B_HEADS, T], F32),
            ("gcum", [P, B_HEADS, T], F32),
            ("z_la", [P, TT, B_KEY], F32),
            ("z_tmp", [P, TT, B_KEY], F32),
            ("ed0", [P, B_HEADS, T], F32),
            ("ed1", [P, B_HEADS, T], F32),
            ("qe0", [P, B_HEADS, T], F32),
            ("qe1", [P, B_HEADS, T], F32),
            ("ke0", [P, B_HEADS, T], F32),
            ("ke1", [P, B_HEADS, T], F32),
            ("score_in", [P, B_HEADS * TT, P], F32),
            ("score_x", [P, B_HEADS, P], F32),
            ("bv", [P, TT, D], F32),
            ("br", [P, TT, D], F32),
            ("bsg", [P, TT, D], F32),
            ("bo", [P, TT, D], F32),
            ("bg_row", [P, B_KEY], F32),
            ("bnorm_row", [P, B_HV], F32),
            ("w_g2", [B_RANK, B_KEY], F32),
            ("w_g", [P, KB, B_RANK], F32),
            ("masks", [P, B_LEVELS + 1, P], U32),
            ("g_lrT", [B_RANK, T], F32),
            ("head_ms", [P, 4, TT * B_HEADS], F32),
        ])
        ed, qe, ke = [ed0, ed1], [qe0, qe1], [ke0, ke1]
        (_, hn, hT) = overlay([("pad_norm", [P, 112 * T], F32), ("hn", [P, TT, D], F32), ("hT", [P, KB, T], F32)])
        (_, final_row) = overlay([("pad_final", [P, 104 * T], F32), ("final_row", [P, D], F32)])

        psum = ctx.enter_context(nc.psum_tensor("psum", [P, 8, BANK], F32))

        raw_loaded = [sem(f"raw_loaded{s}") for s in range(RAW_SLOTS)]
        hi_ready, lo_ready, tile_used = sem("hi_ready"), sem("lo_ready"), sem("tile_used")
        x_loaded, small_loaded, gla_loaded, final_loaded = sem("x_loaded"), sem("small_loaded"), sem("gla_loaded"), sem("final_loaded")
        ws_masked = sem("ws_masked")
        dve_chain, act_chain = sem("dve_chain"), sem("act_chain")
        x_ready = [sem(f"x_ready{i}") for i in range(5)]
        squares = [sem(f"squares{i}") for i in range(5)]
        ms_ready = [sem(f"ms_ready{i}") for i in range(5)]
        rms_ready = [sem(f"rms_ready{i}") for i in range(5)]
        hn_ready = [sem(f"hn_ready{i}") for i in range(5)]
        hn_turned = [sem(f"hn_turned{i}") for i in range(4)]
        hT_ready = [sem(f"hT_ready{i}") for i in range(4)]
        hT_hi_ready = [sem(f"hT_hi_ready{i}") for i in range(4)]
        hT_lo_ready = [sem(f"hT_lo_ready{i}") for i in range(4)]
        ain_biased, ain_gelu = sem("ain_biased"), sem("ain_gelu")
        v_centred, v_squares, v_ms, v_std, v_normed = sem("v_centred"), sem("v_squares"), sem("v_ms"), sem("v_std"), sem("v_normed")
        sv_done, y_ready, y_turned, yT_hi_ready, yT_lo_ready = sem("sv_done"), sem("y_ready"), sem("y_turned"), sem("yT_hi_ready"), sem("yT_lo_ready")
        q_copied = [sem(f"q_copied{l}") for l in range(2)]
        scores_done = [sem(f"scores_done{l}") for l in range(2)]
        scores_copied = [sem(f"scores_copied{l}") for l in range(2)]
        gelu_done = [sem(f"gelu_done{l}") for l in range(2)]
        shifted = [sem(f"shifted{l}") for l in range(2)]
        exps = [sem(f"exps{l}") for l in range(2)]
        gates_ready = [sem(f"gates_ready{l}") for l in range(2)]
        picks_turned = [sem(f"picks_turned{l}") for l in range(2)]
        picksT_ready = [sem(f"picksT_ready{l}") for l in range(2)]
        onehots = [sem(f"onehots{l}") for l in range(2)]
        gmat_done = [sem(f"gmat_done{l}") for l in range(2)]
        gated = [sem(f"gated{l}") for l in range(2)]
        w_hi_ready = [sem(f"w_hi_ready{l}") for l in range(2)]
        w_lo_ready = [sem(f"w_lo_ready{l}") for l in range(2)]
        glr_done, glr_copied, la_done, z_ready, la_abs, la_exp, la_ln, la_ready = (
            sem("glr_done"), sem("glr_copied"), sem("la_done"), sem("z_ready"), sem("la_abs"), sem("la_exp"), sem("la_ln"), sem("la_ready"))
        gcum_done, gcum_copied, qk_copied = sem("gcum_done"), sem("gcum_copied"), sem("qk_copied")
        score_zeroed, diff_ready, decay_ready, qk_decayed, level_done, level_kept = (
            sem("score_zeroed"), sem("diff_ready"), sem("decay_ready"), sem("qk_decayed"), sem("level_done"), sem("level_kept"))
        bv_copied, sig_done, silu_done, o_done, o_squares, o_ms, o_rms, o_ready, o_turned, oT_hi_ready, oT_lo_ready = (
            sem("bv_copied"), sem("sig_done"), sem("silu_done"), sem("o_done"), sem("o_squares"), sem("o_ms"), sem("o_rms"),
            sem("o_ready"), sem("o_turned"), sem("oT_hi_ready"), sem("oT_lo_ready"))
        normed_out, stored = sem("normed_out"), sem("stored")

        def bank_pair(b, n=2):
            return psum[:, b:b + n, :].rearrange("p b c -> p (b c)")

        block = ctx.enter_context(nc.Block())

        @block.sync
        def _(sp):
            sp.dma_start(x[:, :, :], t["x"].rearrange("(h p) d -> p h d", p=P)).then_inc(x_loaded, 16)

            def load(src, slot):
                sp.dma_start(raw[slot][:, :], src).then_inc(raw_loaded[slot], 16)

            def stage(name, first, count):
                if first == 0:
                    for s in range(RAW_SLOTS):
                        load(t[name][s], s)
                    with sp.Fori(1, count // RAW_SLOTS) as i:
                        for s in range(RAW_SLOTS):
                            sp.wait_ge(lo_ready, i * RAW_SLOTS + (s + 1 - RAW_SLOTS))
                            load(t[name][i * RAW_SLOTS + s], s)
                else:
                    with sp.Fori(0, count // RAW_SLOTS) as i:
                        for s in range(RAW_SLOTS):
                            sp.wait_ge(lo_ready, i * RAW_SLOTS + (first + s + 1 - RAW_SLOTS))
                            load(t[name][i * RAW_SLOTS + s], s)

            stage("a_in", AIN, N_AIN)
            stage("a_out", AOUT, N_AOUT)
            for l in range(2):
                stage(f"w_q{l}", WQ[l], N_WQ)
                stage(f"u{l}", UT[l], N_EXP)
                stage(f"v{l}", VT[l], N_EXP)
                if l == 0:
                    stage("b_qk", BQK, N_BQK)
                    stage("b_vr", BVR, N_BVR)
                    stage("b_out", BOUT, N_BOUT)
            for h in range(TT):
                sp.wait_ge(normed_out, h + 1)
                sp.dma_start(out[h], hn[:, h, :]).then_inc(stored, 16)
            sp.wait_ge(stored, 16 * TT)

        @block.gpsimd
        def _(pool):
            small = [(consts[:, :, :], t["consts"]), (gains[:, :, :], t["gains"]),
                     (wsT[:, :, :], t["w_sT"]), (b_sT[:, :], t["b_sT"]),
                     (b_in[:, :], t["b_in"].partition_broadcast(P)),
                     (ln_g[:, :], t["ln_g"].partition_broadcast(P)), (ln_b[:, :], t["ln_b"].partition_broadcast(P)),
                     (keysT[:, :, :, :], t["keysT"])]
            for dst, src in small:
                pool.dma_start(dst, src).then_inc(small_loaded, 16)
            pool.wait_ge(small_loaded, 16 * len(small))
            pool.affine_select(out=wsT[:, :, :], in_=wsT[:, :, :], compare_op=ALU.is_ge, fill=0.0, base=0,
                               pattern=[[0, A_GROUPS], [1, P]], channel_multiplier=-1).then_inc(ws_masked, 1)
            pool.wait_ge(x_ready[2], 4)
            gla = [(masks[:, :, :], t["masks"]), (w_g[:, :, :], t["w_g"]), (w_g2[:, :], t["w_g2"]),
                   (bg_row[:, :], t["b_g"].partition_broadcast(P)), (bnorm_row[:, :], t["b_norm"].partition_broadcast(P))]
            for dst, src in gla:
                pool.dma_start(dst, src).then_inc(gla_loaded, 16)
            pool.memset(score_in[:, :, :], 0.0).then_inc(score_zeroed, 1)
            pool.wait_ge(x_ready[4], 4)
            pool.dma_start(final_row[:, :], t["final_norm"].partition_broadcast(P)).then_inc(final_loaded, 16)

        @block.scalar
        def _(act):
            def hi(slot, raw_count, used):
                act.wait_ge(raw_loaded[slot], raw_count)
                if used is not None:
                    act.wait_ge(tile_used, used)
                act.activation(tile_hi[slot % SPLIT_SLOTS][:, :], raw[slot][:, :], ACT.Copy).then_inc(hi_ready, 1)

            def hi_at(n):
                hi(n % RAW_SLOTS, 16 * (n // RAW_SLOTS + 1), n - 1 if n >= SPLIT_SLOTS else None)

            def hi_in(i, c, first):
                n = first + c
                hi(n % RAW_SLOTS, i * 16 + 16 * (n // RAW_SLOTS + 1), i * RAW_SLOTS + (n - 1))

            chained = [0]

            def norm(i):
                for h in range(TT):
                    if i == 0:
                        act.wait_ge(x_loaded, 16)
                    else:
                        act.wait_ge(x_ready[i], 2 * h + 2)
                    act.activation(hn[:, h, :], x[:, h, :], ACT.Square, accum_out=sumsq[:, h:h + 1]).then_inc(squares[i], 1)
                for h in range(TT):
                    act.wait_ge(ms_ready[i], h + 1)
                    act.activation(rms[:, h:h + 1], meansq[:, h:h + 1], ACT.Sqrt).then_inc(rms_ready[i], 1)
                if i == 4:
                    return
                for h in range(TT):
                    act.wait_ge(hT_ready[i], h + 1)
                    act.activation(hT_hi[:, :, h * P:(h + 1) * P], hT[:, :, h * P:(h + 1) * P], ACT.Copy).then_inc(hT_hi_ready[i], 1)

            hi_at(0)
            hi_at(1)
            norm(0)

            def a_gelu(j):
                for h in range(TT):
                    act.wait_ge(ain_biased, 2 * TT * j + 2 * h + 2)
                    if j < 2:
                        z = zv[:, h, j * TILE:(j + 1) * TILE]
                        act.activation(z, z, ACT.Gelu, accum_out=v_sum[:, h, j:j + 1]).then_inc(ain_gelu, 1)
                    else:
                        z = zu[:, h, (j - 2) * TILE:(j - 1) * TILE]
                        act.activation(z, z, ACT.Gelu).then_inc(ain_gelu, 1)

            for n in range(2, AOUT + 2):
                hi_at(n)
                j = (n - 2) // KB - 1
                if (n - 2) % KB == 0 and 0 <= j < 3:
                    a_gelu(j)
                if n in (2 * KB + 4, 2 * KB + 5):
                    h = n - 2 * KB - 4
                    act.wait_ge(v_centred, h + 1)
                    act.activation(yT_hi[:, 8 * h:8 * h + 8, :].rearrange("p a b -> p (a b)"), zv[:, h, :],
                                   ACT.Square, accum_out=sumsq[:, h:h + 1]).then_inc(v_squares, 1)
                if n == 2 * KB + 7:
                    act.wait_ge(v_ms, 1)
                    act.activation(rms[:, :], meansq[:, :], ACT.Sqrt).then_inc(v_std, 1)
            a_gelu(3)
            for h in range(TT):
                act.wait_ge(y_turned, h + 1)
                for c in range(4):
                    act.activation(yT_hi[:, 4 * c:4 * c + 4, h * P:(h + 1) * P],
                                   psum[:, 4 * h + c, :].rearrange("p (a b) -> p a b", a=4), ACT.Copy).then_inc(yT_hi_ready, 1)
            for n in range(AOUT + 2, WQ[0] + 2):
                hi_at(n)

            def peer(l):
                norm(1 + 2 * l)
                with act.Fori(0, N_WQ // RAW_SLOTS) as i:
                    for c in range(RAW_SLOTS):
                        hi_in(i, c, WQ[l] + 2)
                        act.wait_ge(tile_used, i * RAW_SLOTS + (WQ[l] + c + 1))
                        act.activation(qT[:, i * RAW_SLOTS + c, :], psum[:, c, 0:T], ACT.Copy).then_inc(q_copied[l], 1)
                for h in range(TT):
                    for c in range(4):
                        act.wait_ge(scores_done[l], 4 * h + c + 1)
                        act.activation(scores[:, h, 4 * c:4 * c + 4, :].rearrange("p a b -> p (a b)"), psum[:, 4 * h + c, :],
                                       ACT.Copy).then_inc(scores_copied[l], 1)

                def expert_acts(first, last):
                    with act.Fori(first // RAW_SLOTS, last // RAW_SLOTS) as i:
                        for c in range(RAW_SLOTS):
                            hi_in(i, c, UT[l] + 2)
                            act.wait_ge(tile_used, i * RAW_SLOTS + (UT[l] + c + 1))
                            act.activation(acts[:, i * RAW_SLOTS + c, :], psum[:, c, 0:T], ACT.Gelu).then_inc(gelu_done[l], 1)

                act.preload_act_table(ACT.Gelu)
                expert_acts(0, 76)
                for h in range(TT):
                    act.wait_ge(shifted[l], h + 1)
                    act.activation(picks[:, h, 2, :], picks[:, h, 2, :], ACT.Exp).then_inc(exps[l], 1)
                act.preload_act_table(ACT.Gelu)
                expert_acts(76, N_EXP)
                act.wait_ge(picks_turned[l], 1)
                act.activation(picksT[:, 0:2, :].rearrange("p a b -> p (a b)"), psum[:, 4, :], ACT.Copy).then_inc(picksT_ready[l], 1)
                act.activation(picksT[:, 2, :], psum[:, 5, 0:T], ACT.Copy).then_inc(picksT_ready[l], 1)

                def gated_hi(k, slot, used):
                    if used is not None:
                        act.wait_ge(tile_used, used)
                    act.activation(w_hi[slot][:, :], acts[:, k, :], ACT.Copy).then_inc(w_hi_ready[l], 1)

                act.wait_ge(gated[l], T // 4)
                gated_hi(0, 0, None)
                gated_hi(1, 1, None)
                with act.Fori(0, N_EXP // RAW_SLOTS - 1) as i:
                    for c in range(RAW_SLOTS):
                        hi_in(i, c, VT[l] + 2)
                        gated_hi(i * RAW_SLOTS + (c + 2), c % 2, i * RAW_SLOTS + (VT[l] + c + 1))
                for k in (N_EXP - 2, N_EXP - 1):
                    hi_at(VT[l] + k)
                    gated_hi(k, k % 2, VT[l] + k - 1)

            peer(0)
            hi_at(BQK)
            hi_at(BQK + 1)
            norm(2)
            act.wait_ge(glr_done, 1)
            act.activation(g_lrT[:, :], psum[0:B_RANK, 4, 0:T], ACT.Copy).then_inc(glr_copied, 1)
            for n in range(BQK + 2, BVR + 2):
                hi_at(n)
                c = n - 2 - BQK
                act.wait_ge(tile_used, BQK + c + 1)
                if c < B_HEADS:
                    act.activation(gq[:, c, :], psum[:, c % 4, 0:T], ACT.Copy, scale=float(B_HK) ** -0.5).then_inc(qk_copied, 1)
                else:
                    act.activation(gk[:, c - B_HEADS, :], psum[:, c % 4, 0:T], ACT.Copy).then_inc(qk_copied, 1)
                if c == 1:
                    act.wait_ge(z_ready, 1)
                    act.activation(z_tmp[:, :, :], z_la[:, :, :], ACT.Abs).then_inc(la_abs, 1)
                    act.wait_ge(la_abs, 1)
                    act.activation(z_tmp[:, :, :], z_tmp[:, :, :], ACT.Exp, scale=-1.0).then_inc(la_exp, 1)
                    act.wait_ge(la_exp, 1)
                    act.activation(z_tmp[:, :, :], z_tmp[:, :, :], ACT.Ln, bias=1.0).then_inc(la_ln, 1)
            act.wait_ge(gcum_done, 1)
            act.activation(gcum[:, :, :].rearrange("p a b -> p (a b)"), bank_pair(5), ACT.Copy).then_inc(gcum_copied, 1)

            def decay(L):
                act.wait_ge(diff_ready, L)
                act.activation(ed[L % 2][:, :, :], ed[L % 2][:, :, :], ACT.Exp).then_inc(decay_ready, 1)

            decay(1)
            for n in range(BVR + 2, BOUT + 2):
                hi_at(n)
                c = n - 2 - BVR
                if c % 2 == 0 and c // 2 + 2 <= B_LEVELS + 1:
                    decay(c // 2 + 2)
                if c == KB - 1:
                    for b in range(4):
                        act.wait_ge(tile_used, BVR + KB)
                        act.activation(bv[:, b // 2, (b % 2) * BANK:(b % 2 + 1) * BANK], psum[:, b, :], ACT.Copy).then_inc(bv_copied, 1)
            for h in range(TT):
                act.wait_ge(tile_used, BOUT)
                act.activation(bsg[:, h, :], bank_pair(2 * h), ACT.Sigmoid).then_inc(sig_done, 1)
            for h in range(TT):
                act.wait_ge(o_done, h + 1)
                act.activation(bo[:, h, :], bank_pair(2 * h), ACT.Square).then_inc(o_squares, 1)
            act.wait_ge(o_ms, 1)
            act.activation(head_ms[:, 2, :], head_ms[:, 1, :], ACT.Sqrt).then_inc(o_rms, 1)
            for h in range(TT):
                act.wait_ge(o_turned, h + 1)
                act.activation(hT_hi[:, :, h * P:(h + 1) * P], bank_pair(4 + 2 * h).rearrange("p (a b) -> p a b", a=KB),
                               ACT.Copy).then_inc(oT_hi_ready, 1)
            for n in range(BOUT + 2, WQ[1] + 2):
                hi_at(n)
            peer(1)
            norm(4)

        @block.vector
        def _(dve):
            def lo(slot, ready):
                dve.wait_ge(hi_ready, ready)
                s = slot % SPLIT_SLOTS
                dve.tensor_tensor(tile_lo[s][:, :], raw[slot][:, :], tile_hi[s][:, :].bitcast(F32),
                                  ALU.subtract).then_inc(lo_ready, 1)

            def lo_at(n):
                lo(n % RAW_SLOTS, n + 1)

            def lo_in(i, c, first):
                lo((first + c) % RAW_SLOTS, i * RAW_SLOTS + (first + c + 1))

            chain = [0]

            def did(ins):
                ins.then_inc(dve_chain, 1)
                chain[0] += 1
                return chain[0]

            def after(number):
                dve.wait_ge(dve_chain, number)

            def norm(i):
                for h in range(TT):
                    dve.wait_ge(squares[i], h + 1)
                    dve.tensor_scalar(meansq[:, h:h + 1], sumsq[:, h:h + 1], 1.0 / D, EPS, ALU.mult, ALU.add).then_inc(ms_ready[i], 1)
                for h in range(TT):
                    dve.wait_ge(rms_ready[i], h + 1)
                    after(did(dve.reciprocal(rstd[:, h:h + 1], rms[:, h:h + 1])))
                    ins = dve.tensor_scalar(hn[:, h, :], x[:, h, :], rstd[:, h:h + 1], None, ALU.mult)
                    ins.then_inc(hn_ready[i], 1)
                    if i == 4:
                        dve.wait_ge(hn_ready[4], h + 1)
                        dve.wait_ge(final_loaded, 16)
                        dve.tensor_tensor(hn[:, h, :], hn[:, h, :], final_row[:, :], ALU.mult).then_inc(normed_out, 1)
                if i == 4:
                    return
                for h in range(TT):
                    dve.wait_ge(hn_turned[i], h + 1)
                    cols = slice(h * P, (h + 1) * P)
                    dve.tensor_tensor(hT[:, :, cols], bank_pair(2 * h).rearrange("p (a b) -> p a b", a=KB),
                                      gains[:, i, :].unsqueeze(2).broadcast_to([P, KB, P]), ALU.mult).then_inc(hT_ready[i], 1)
                for h in range(TT):
                    dve.wait_ge(hT_hi_ready[i], h + 1)
                    cols = slice(h * P, (h + 1) * P)
                    dve.tensor_tensor(hT_lo[:, :, cols], hT[:, :, cols], hT_hi[:, :, cols].bitcast(F32),
                                      ALU.subtract).then_inc(hT_lo_ready[i], 1)

            def add_to_x(i, first_bank, last_tile):
                dve.wait_ge(tile_used, last_tile + 1)
                for b in range(4):
                    part = x[:, b // 2, (b % 2) * BANK:(b % 2 + 1) * BANK]
                    dve.tensor_tensor(part, psum[:, first_bank + b, :], part, ALU.add).then_inc(x_ready[i], 1)

            lo_at(0)
            lo_at(1)
            dve.wait_ge(small_loaded, 16 * 8)
            norm(0)

            def a_bias(j):
                dve.wait_ge(tile_used, (j + 1) * KB)
                for b in range(4):
                    h, cols = b // 2, (j % 2) * TILE + (b % 2) * BANK
                    z = zv if j < 2 else zu
                    dve.tensor_tensor(z[:, h, cols:cols + BANK], psum[:, 4 * (j % 2) + b, :],
                                      b_in[:, j * TILE + (b % 2) * BANK:j * TILE + (b % 2 + 1) * BANK], ALU.add).then_inc(ain_biased, 1)

            for n in range(2, AOUT + 2):
                lo_at(n)
                if (n - 1) % KB == 0 and n > KB:
                    a_bias((n - 1) // KB - 1)
                step = n - 2 * KB
                if step == 3:
                    dve.wait_ge(ain_gelu, 4)
                    after(did(dve.tensor_tensor(v_mean[:, :], v_sum[:, :, 0], v_sum[:, :, 1], ALU.add)))
                    after(did(dve.tensor_scalar(v_mean[:, :], v_mean[:, :], 1.0 / A_WIDTH, None, ALU.mult)))
                    for h in range(TT):
                        dve.tensor_scalar(zv[:, h, :], zv[:, h, :], v_mean[:, h:h + 1], None, ALU.subtract).then_inc(v_centred, 1)
                if step == 6:
                    dve.wait_ge(v_squares, TT)
                    dve.tensor_scalar(meansq[:, :], sumsq[:, :], 1.0 / A_WIDTH, EPS, ALU.mult, ALU.add).then_inc(v_ms, 1)
                if step == 8:
                    dve.wait_ge(v_std, 1)
                    after(did(dve.reciprocal(rstd[:, :], rms[:, :])))
                if step in (10, 12):
                    h = (step - 10) // 2
                    normed_v = did(dve.scalar_tensor_tensor(zv[:, h, :], zv[:, h, :], rstd[:, h:h + 1], ln_g[:, :], ALU.mult, ALU.mult))
                if step in (11, 13):
                    h = (step - 11) // 2
                    after(normed_v)
                    dve.tensor_tensor(zv[:, h, :], zv[:, h, :], ln_b[:, :], ALU.add).then_inc(v_normed, 1)
            dve.wait_ge(ain_gelu, 8)
            for h in range(TT):
                dve.wait_ge(sv_done, h + 1)
                for g in range(A_GROUPS):
                    u = zu[:, h, g * A_GDIM:(g + 1) * A_GDIM]
                    bank, col = 4 * h + g // 2, (g % 2) * A_GDIM
                    dve.scalar_tensor_tensor(u, psum[:, bank, col:col + A_GDIM], b_sT[:, g:g + 1], u,
                                             ALU.add, ALU.mult).then_inc(y_ready, 1)
            for h in range(TT):
                for c in range(4):
                    dve.wait_ge(yT_hi_ready, 4 * h + c + 1)
                    dst = (slice(None), slice(4 * c, 4 * c + 4), slice(h * P, (h + 1) * P))
                    dve.tensor_tensor(yT_lo[dst], psum[:, 4 * h + c, :].rearrange("p (a b) -> p a b", a=4),
                                      yT_hi[dst].bitcast(F32), ALU.subtract).then_inc(yT_lo_ready, 1)
            for n in range(AOUT + 2, WQ[0] + 2):
                lo_at(n)
            add_to_x(1, 0, WQ[0] - 1)

            def top16(rows, values, places, between):
                n8 = [did(dve.max(values[r][:, 0:8], rows[r])) for r in range(2)]
                for r in range(2):
                    after(n8[r])
                    n8[r] = did(dve.max_index(places[r][:, 0:8], values[r][:, 0:8], rows[r]))
                if between:
                    between[0]()
                for r in range(2):
                    after(n8[r])
                    n8[r] = did(dve.match_replace(rows[r], values[r][:, 0:8], rows[r], LOWEST))
                for r in range(2):
                    after(n8[r])
                    n8[r] = did(dve.max(values[r][:, 8:16], rows[r]))
                if len(between) > 1:
                    between[1]()
                for r in range(2):
                    after(n8[r])
                    n8[r] = did(dve.max_index(places[r][:, 8:16], values[r][:, 8:16], rows[r]))
                return n8[1]

            def peer(l):
                norm(1 + 2 * l)
                with dve.Fori(0, N_WQ // RAW_SLOTS) as i:
                    for c in range(RAW_SLOTS):
                        lo_in(i, c, WQ[l] + 2)
                n = UT[l] + 2
                dve.wait_ge(scores_copied[l], 4 * TT)
                for h in range(TT):
                    for r in range(0, P_ROWS, 2):
                        lo_at(n)
                        top16([scores[:, h, r + k, :] for k in range(2)], [topv[:, h, r + k, :] for k in range(2)],
                              [topi[:, h, r + k, :] for k in range(2)], [lambda: lo_at(n + 1)])
                        n += 2
                for h in range(TT):
                    lo_at(n)
                    n += 1
                    after(chain[0])
                    v1 = topv[:, h, 0:P_ROWS:2, :].unsqueeze(3).broadcast_to([P, P_HEADS, TOPK, TOPK])
                    v2 = topv[:, h, 1:P_ROWS:2, :].unsqueeze(2).broadcast_to([P, P_HEADS, TOPK, TOPK])
                    sums = did(dve.tensor_tensor(cand[:, :, :].rearrange("p g (a b) -> p g a b", a=TOPK), v1, v2, ALU.add))
                    after(sums)
                    for g in range(0, P_HEADS, 2):
                        lo_at(n)
                        top16([cand[:, g + k, :] for k in range(2)], [candv[:, g + k, :] for k in range(2)],
                              [candpos[:, g + k, :] for k in range(2)], [lambda: lo_at(n + 1), lambda: lo_at(n + 2)])
                        n += 3
                    lo_at(n)
                    n += 1
                    after(chain[0])
                    a1 = did(dve.tensor_scalar(pos_a[:, :, :], candpos[:, :, :], 4, None, ALU.logical_shift_right))
                    a2 = did(dve.tensor_scalar(pos_b[:, :, :], candpos[:, :, :], 15, None, ALU.bitwise_and))
                    a3 = did(dve.tensor_copy(topi_f[:, :, :], topi[:, h, :, :]))
                    after(a1)
                    a1 = did(dve.tensor_copy(pos_af[:, :, :], pos_a[:, :, :]))
                    after(a2)
                    a2 = did(dve.tensor_copy(pos_bf[:, :, :], pos_b[:, :, :]))
                    after(a3)
                    for half, pos in ((0, pos_af), (1, pos_bf)):
                        after((a1, a2)[half])
                        lo_at(n)
                        want = pos[:, :, :].unsqueeze(3).broadcast_to([P, P_HEADS, TOPK, TOPK])
                        ranks = iota[:, 0:TOPK].unsqueeze(1).unsqueeze(1).broadcast_to([P, P_HEADS, TOPK, TOPK])
                        numbers = topi_f[:, half:P_ROWS:2, :].unsqueeze(2).broadcast_to([P, P_HEADS, TOPK, TOPK])
                        eq = did(dve.tensor_tensor(look[:, :, :, :], want, ranks, ALU.is_equal))
                        lo_at(n + 1)
                        after(eq)
                        eq = did(dve.tensor_tensor(look[:, :, :, :], look[:, :, :, :], numbers, ALU.mult))
                        lo_at(n + 2)
                        after(eq)
                        eq = did(dve.tensor_reduce(picks[:, h, half, :].rearrange("p (g k) -> p g k", g=P_HEADS),
                                                   look[:, :, :, :], AX.X, ALU.add))
                        after(eq)
                        n += 3
                    dve.tensor_tensor(picks[:, h, 2, :].rearrange("p (g k) -> p g k", g=P_HEADS), candv[:, :, :],
                                      candv[:, :, 0:1].broadcast_to([P, P_HEADS, TOPK]), ALU.subtract).then_inc(shifted[l], 1)
                    dve.wait_ge(shifted[l], h + 1)
                while n < UT[l] + 2 + 80:
                    lo_at(n)
                    n += 1
                for h in range(TT):
                    e = picks[:, h, 2, :].rearrange("p (g k) -> p g k", g=P_HEADS)
                    dve.wait_ge(exps[l], h + 1)
                    after(did(dve.tensor_reduce(head_sum[:, h, :], e, AX.X, ALU.add)))
                    after(did(dve.reciprocal(head_inv[:, h, :], head_sum[:, h, :])))
                    dve.tensor_tensor(e, e, head_inv[:, h, :].unsqueeze(2).broadcast_to([P, P_HEADS, TOPK]),
                                      ALU.mult).then_inc(gates_ready[l], 1)
                with dve.Fori(0, (N_EXP - 80) // RAW_SLOTS) as i:
                    for c in range(RAW_SLOTS):
                        lo_in(i, c, UT[l] + 2 + 80)

                def onehots_of(token0, g):
                    for c in range(4):
                        s = 4 * (g % 2) + c
                        dve.tensor_scalar(onehot1[:, s, :], iota, picksT[:, 0, bass.ds(token0 + c, 1)], None, ALU.is_equal)
                        ins = dve.tensor_scalar(onehot2[:, s, :], iota, picksT[:, 1, bass.ds(token0 + c, 1)],
                                                picksT[:, 2, bass.ds(token0 + c, 1)], ALU.is_equal, ALU.mult)
                    ins.then_inc(onehots[l], 1)

                def gate(token0, g):
                    a = acts[:, :, bass.ds(token0, 4)].rearrange("p i t -> p t i")
                    dve.tensor_tensor(a, psum[:, g % 4, :].rearrange("p (t i) -> p t i", t=4), a, ALU.mult).then_inc(gated[l], 1)

                groups = T // 4
                dve.wait_ge(picksT_ready[l], 2)
                dve.wait_ge(gelu_done[l], N_EXP)
                onehots_of(0, 0)
                onehots_of(4, 1)
                with dve.Fori(0, groups // 4 - 1) as i:
                    for c in range(4):
                        dve.wait_ge(gmat_done[l], i * 4 + (c + 1))
                        gate(i * 16 + 4 * c, c)
                        onehots_of(i * 16 + (4 * c + 8), c)
                for g in range(groups - 4, groups):
                    dve.wait_ge(gmat_done[l], g + 1)
                    gate(4 * g, g)
                    if g + 2 < groups:
                        onehots_of(4 * (g + 2), g)

                def gated_lo(k, slot, ready):
                    dve.wait_ge(w_hi_ready[l], ready)
                    dve.tensor_tensor(w_lo[slot][:, :], acts[:, k, :], w_hi[slot][:, :].bitcast(F32), ALU.subtract).then_inc(w_lo_ready[l], 1)

                dve.wait_ge(gated[l], groups)
                gated_lo(0, 0, 1)
                gated_lo(1, 1, 2)
                with dve.Fori(0, N_EXP // RAW_SLOTS - 1) as i:
                    for c in range(RAW_SLOTS):
                        lo_in(i, c, VT[l] + 2)
                        gated_lo(i * RAW_SLOTS + (c + 2), c % 2, i * RAW_SLOTS + (c + 3))
                for k in (N_EXP - 2, N_EXP - 1):
                    lo_at(VT[l] + k)
                    gated_lo(k, k % 2, k + 1)

            peer(0)
            lo_at(BQK)
            lo_at(BQK + 1)
            add_to_x(2, 4, BQK - 1)
            norm(2)
            for n in range(BQK + 2, BVR + 2):
                lo_at(n)
                c = n - 2 - BQK
                if c == 0:
                    dve.wait_ge(la_done, TT)
                    dve.wait_ge(gla_loaded, 16 * 5)
                    dve.tensor_tensor(z_la[:, :, :], psum[:, 5:7, :], bg_row[:, :].unsqueeze(1).broadcast_to([P, TT, B_KEY]),
                                      ALU.add).then_inc(z_ready, 1)
                if c == 2:
                    dve.wait_ge(la_ln, 1)
                    dve.scalar_tensor_tensor(z_la[:, :, :].rearrange("p a b -> p (a b)"), z_la[:, :, :].rearrange("p a b -> p (a b)"), 0.0,
                                             z_tmp[:, :, :].rearrange("p a b -> p (a b)"), ALU.min, ALU.subtract).then_inc(la_ready, 1)

            def diff(L):
                e, flat = ed[L % 2], gcum
                if L == 1:
                    last = gcum[:, :, P - 1:P].broadcast_to([P, B_HEADS, P])
                    dve.tensor_tensor(e[:, :, 0:P], last, gcum[:, :, 0:P], ALU.subtract)
                    dve.tensor_copy(e[:, :, P:T], gcum[:, :, P:T]).then_inc(diff_ready, 1)
                    return
                m = 1 << (L - 2)
                g4 = gcum[:, :, :].rearrange("p h (b w m) -> p (h b) w m", w=2, m=m)
                e4 = e[:, :, :].rearrange("p h (b w m) -> p (h b) w m", w=2, m=m)
                ref = g4[:, :, 0, m - 1:m].broadcast_to([P, B_HEADS * T // (2 * m), m])
                dve.tensor_tensor(e4[:, :, 0, :], ref, g4[:, :, 0, :], ALU.subtract)
                dve.tensor_tensor(e4[:, :, 1, :], g4[:, :, 1, :], ref, ALU.subtract).then_inc(diff_ready, 1)

            def decayed(L):
                if L == 0:
                    dve.wait_ge(qk_copied, 2 * B_HEADS)
                    return
                dve.wait_ge(decay_ready, L)
                if L >= 3:
                    dve.wait_ge(level_done, L - 1)
                dve.tensor_tensor(qe[L % 2][:, :, :], gq[:, :, :], ed[L % 2][:, :, :], ALU.mult)
                dve.tensor_tensor(ke[L % 2][:, :, :], gk[:, :, :], ed[L % 2][:, :, :], ALU.mult).then_inc(qk_decayed, 1)

            def keep(L):
                dve.wait_ge(level_done, L + 1)
                if L == 1:
                    dve.tensor_copy(score_x[:, :, :].rearrange("p a b -> p (a b)"), psum[:, 6, :]).then_inc(level_kept, 1)
                    return
                mask = masks[:, B_LEVELS if L == 0 else L - 2, :].unsqueeze(1).broadcast_to([P, B_HEADS * TT, P])
                dve.copy_predicated(score_in[:, :, :], mask,
                                    bank_pair(4 + 2 * (L % 2)).rearrange("p (a b) -> p a b", b=P)).then_inc(level_kept, 1)

            dve.wait_ge(gcum_copied, 1)
            decayed(0)
            diff(1)
            dve.wait_ge(score_zeroed, 1)
            levels = B_LEVELS + 2
            for n in range(BVR + 2, BOUT + 2):
                lo_at(n)
                c = n - 2 - BVR
                if c % 2 == 0:
                    if c // 2 + 2 < levels:
                        if c // 2 >= 1:
                            dve.wait_ge(qk_decayed, c // 2)
                        diff(c // 2 + 2)
                    decayed(c // 2 + 1)
                else:
                    if c > 1:
                        dve.wait_ge(level_kept, c // 2)
                    keep(c // 2)
            dve.wait_ge(level_kept, levels - 1)
            keep(levels - 1)
            for h in range(TT):
                dve.wait_ge(sig_done, h + 1)
                dve.tensor_tensor(br[:, h, :], bank_pair(2 * h), bsg[:, h, :], ALU.mult).then_inc(silu_done, 1)
            for h in range(TT):
                dve.wait_ge(o_squares, h + 1)
                last = did(dve.tensor_reduce(head_ms[:, 0, B_HEADS * h:B_HEADS * (h + 1)],
                                             bo[:, h, :].rearrange("p (g v) -> p g v", g=B_HEADS), AX.X, ALU.add))
            after(last)
            dve.tensor_scalar(head_ms[:, 1, :], head_ms[:, 0, :], 1.0 / B_HV, EPS, ALU.mult, ALU.add).then_inc(o_ms, 1)
            dve.wait_ge(o_rms, 1)
            after(did(dve.reciprocal(head_ms[:, 3, :], head_ms[:, 2, :])))
            for h in range(TT):
                o3 = bo[:, h, :].rearrange("p (g v) -> p g v", g=B_HEADS)
                inv = head_ms[:, 3, B_HEADS * h:B_HEADS * (h + 1)].unsqueeze(2).broadcast_to([P, B_HEADS, B_HV])
                after(did(dve.tensor_tensor(o3, bank_pair(2 * h).rearrange("p (g v) -> p g v", g=B_HEADS), inv, ALU.mult)))
                after(did(dve.tensor_tensor(o3, o3, bnorm_row[:, :].unsqueeze(1).broadcast_to([P, B_HEADS, B_HV]), ALU.mult)))
                dve.wait_ge(silu_done, h + 1)
                dve.tensor_tensor(bo[:, h, :], bo[:, h, :], br[:, h, :], ALU.mult).then_inc(o_ready, 1)
            for h in range(TT):
                dve.wait_ge(oT_hi_ready, h + 1)
                cols = slice(h * P, (h + 1) * P)
                dve.tensor_tensor(hT_lo[:, :, cols], bank_pair(4 + 2 * h).rearrange("p (a b) -> p a b", a=KB),
                                  hT_hi[:, :, cols].bitcast(F32), ALU.subtract).then_inc(oT_lo_ready, 1)
            for n in range(BOUT + 2, WQ[1] + 2):
                lo_at(n)
            add_to_x(3, 0, WQ[1] - 1)
            peer(1)
            add_to_x(4, 4, TILES - 1)
            norm(4)

        @block.tensor
        def _(pe):
            def product(o, a, b, start=False, stop=False):
                return pe.matmul(o, a, b, start=start, stop=stop, skip_group_check=True)

            def stationary_tile(slot, ready, bank):
                w_h, w_l = tile_hi[slot], tile_lo[slot]
                o = psum[:, bank, 0:T]
                pe.wait_ge(hi_ready, ready)
                for kb in range(KB):
                    w = w_h[:, kb * P:(kb + 1) * P]
                    product(o, w, hT_hi[:, kb, :], start=kb == 0)
                    product(o, w, hT_lo[:, kb, :])
                pe.wait_ge(lo_ready, ready)
                for kb in range(KB):
                    ins = product(o, w_l[:, kb * P:(kb + 1) * P], hT_hi[:, kb, :], stop=kb == KB - 1)
                ins.then_inc(tile_used, 1)

            def moving_tile(slot, ready, first_bank, a_hi, a_lo, start, stop):
                pe.wait_ge(hi_ready, ready)
                for h in range(TT):
                    cols = slice(h * P, (h + 1) * P)
                    for a, first in ((a_hi, start), (a_lo, False)):
                        for d in range(2):
                            product(psum[:, first_bank + 2 * h + d, :], a[:, cols], tile_hi[slot][:, d * BANK:(d + 1) * BANK], start=first)
                pe.wait_ge(lo_ready, ready)
                for h in range(TT):
                    cols = slice(h * P, (h + 1) * P)
                    for d in range(2):
                        ins = product(psum[:, first_bank + 2 * h + d, :], a_hi[:, cols], tile_lo[slot][:, d * BANK:(d + 1) * BANK], stop=stop)
                ins.then_inc(tile_used, 1)

            def turn(src, first_bank, blocks):
                for b in range(blocks):
                    ins = pe.transpose(psum[:, first_bank + b // 4, (b % 4) * P:(b % 4 + 1) * P], src[:, b * P:(b + 1) * P], ident)
                return ins

            def norm(i):
                for h in range(TT):
                    pe.wait_ge(hn_ready[i], h + 1)
                    turn(hn[:, h, :], 2 * h, KB).then_inc(hn_turned[i], 1)

            pe.wait_ge(small_loaded, 16 * 8)
            norm(0)
            pe.wait_ge(hT_lo_ready[0], TT)
            for j in range(A_BLOCKS):
                if j >= 2:
                    pe.wait_ge(ain_biased, 4 * (j - 1))
                for kb in range(KB):
                    n = AIN + j * KB + kb
                    moving_tile(n % 2, n + 1, 4 * (j % 2), hT_hi[:, kb, :], hT_lo[:, kb, :], kb == 0, kb == KB - 1)
            pe.wait_ge(v_normed, TT)
            pe.wait_ge(ws_masked, 1)
            for h in range(TT):
                pe.wait_ge(ain_biased, 4 * (3 + h))
                for g in range(A_GROUPS):
                    ins = product(psum[:, 4 * h + g // 2, (g % 2) * A_GDIM:(g % 2 + 1) * A_GDIM], wsT[:, g, :],
                                  zv[:, h, g * A_GDIM:(g + 1) * A_GDIM], start=True, stop=True)
                ins.then_inc(sv_done, 1)
            for h in range(TT):
                pe.wait_ge(y_ready, A_GROUPS * (h + 1))
                turn(zu[:, h, :], 4 * h, YB).then_inc(y_turned, 1)
            pe.wait_ge(yT_lo_ready, 4 * TT)
            for kb in range(YB):
                n = AOUT + kb
                moving_tile(n % 2, n + 1, 0, yT_hi[:, kb, :], yT_lo[:, kb, :], kb == 0, kb == YB - 1)

            def peer(l):
                norm(1 + 2 * l)
                pe.wait_ge(hT_lo_ready[1 + 2 * l], TT)
                for c in range(RAW_SLOTS):
                    n = WQ[l] + c
                    stationary_tile(n % 2, n + 1, c)
                with pe.Fori(1, N_WQ // RAW_SLOTS) as i:
                    for c in range(RAW_SLOTS):
                        pe.wait_ge(q_copied[l], i * RAW_SLOTS + (c + 1 - RAW_SLOTS))
                        stationary_tile(c % 2, i * RAW_SLOTS + (WQ[l] + c + 1), c)
                pe.wait_ge(q_copied[l], N_WQ)
                for h in range(TT):
                    for r in range(P_ROWS):
                        ins = product(psum[:, 4 * h + r // 4, (r % 4) * NK:(r % 4 + 1) * NK], qT[:, r, h * P:(h + 1) * P],
                                      keysT[:, l, r % 2, :], start=True, stop=True)
                        if r % 4 == 3:
                            ins.then_inc(scores_done[l], 1)
                for c in range(RAW_SLOTS):
                    pe.wait_ge(scores_copied[l], c + 1)
                    stationary_tile(c % 2, UT[l] + c + 1, c)
                with pe.Fori(1, N_EXP // RAW_SLOTS) as i:
                    for c in range(RAW_SLOTS):
                        pe.wait_ge(gelu_done[l], i * RAW_SLOTS + (c + 1 - RAW_SLOTS))
                        stationary_tile(c % 2, i * RAW_SLOTS + (UT[l] + c + 1), c)
                pe.wait_ge(scores_copied[l], 4 * TT)
                pe.wait_ge(gates_ready[l], TT)
                for k in range(3):
                    for h in range(TT):
                        c = 2 * k + h
                        ins = pe.transpose(psum[:, 4 + c // 4, (c % 4) * P:(c % 4 + 1) * P], picks[:, h, k, :], ident)
                ins.then_inc(picks_turned[l], 1)

                def gmat(g, ready):
                    pe.wait_ge(onehots[l], ready)
                    for c in range(4):
                        s = 4 * (g % 2) + c
                        ins = product(psum[:, g % 4, c * P:(c + 1) * P], onehot1[:, s, :], onehot2[:, s, :], start=True, stop=True)
                    ins.then_inc(gmat_done[l], 1)

                pe.wait_ge(gelu_done[l], N_EXP)
                for g in range(4):
                    gmat(g, g + 1)
                with pe.Fori(1, T // 16) as i:
                    for c in range(4):
                        pe.wait_ge(gated[l], i * 4 + (c - 3))
                        gmat(c, i * 4 + (c + 1))

                def value_tile(slot, ready, k, start, stop):
                    pe.wait_ge(w_lo_ready[l], k + 1)
                    moving_tile(slot, ready, 4, w_hi[slot], w_lo[slot], start, stop)

                for k in range(RAW_SLOTS):
                    value_tile(k % 2, VT[l] + k + 1, k, k == 0, False)
                with pe.Fori(1, N_EXP // RAW_SLOTS - 1) as i:
                    for c in range(RAW_SLOTS):
                        value_tile(c % 2, i * RAW_SLOTS + (VT[l] + c + 1), i * RAW_SLOTS + c, False, False)
                for k in range(N_EXP - RAW_SLOTS, N_EXP):
                    value_tile(k % 2, VT[l] + k + 1, k, False, k == N_EXP - 1)

            peer(0)
            norm(2)
            pe.wait_ge(hT_lo_ready[2], TT)
            pe.wait_ge(gla_loaded, 16 * 5)
            for kb in range(KB):
                ins = product(psum[0:B_RANK, 4, 0:T], w_g[:, kb, :], hT[:, kb, :], start=kb == 0, stop=kb == KB - 1)
            ins.then_inc(glr_done, 1)
            for c in range(N_BQK):
                n = BQK + c
                if c >= 4:
                    pe.wait_ge(qk_copied, c - 3)
                stationary_tile(n % 2, n + 1, c % 4)
                if c == 0:
                    pe.wait_ge(glr_copied, 1)
                    for h in range(TT):
                        product(psum[:, 5 + h, :], g_lrT[:, h * P:(h + 1) * P], w_g2[:, :], start=True, stop=True).then_inc(la_done, 1)
                if c == 5:
                    pe.wait_ge(la_ready, 1)
                    for d in range(B_HEADS):
                        for h in range(TT):
                            ins = product(psum[:, 5 + d // 2, (d % 2) * T + h * P:(d % 2) * T + (h + 1) * P],
                                          z_la[:, h, d * B_HK:(d + 1) * B_HK], tri16, start=True, stop=True)
                    ins.then_inc(gcum_done, 1)

            def level(L):
                q, k = (gq, gk) if L == 0 else (qe[L % 2], ke[L % 2])
                if L == 0:
                    pe.wait_ge(qk_copied, 2 * B_HEADS)
                else:
                    pe.wait_ge(qk_decayed, L)
                if L == 1:
                    pe.wait_ge(gcum_copied, 1)
                if L >= 2:
                    pe.wait_ge(level_kept, L - 1)
                first = 4 + 2 * (L % 2)
                for d in range(B_HEADS):
                    if L == 1:
                        ins = product(psum[:, first, d * P:(d + 1) * P], k[:, d, 0:P], q[:, d, P:T], start=True, stop=True)
                        continue
                    for h in range(TT):
                        c = TT * d + h
                        ins = product(psum[:, first + c // 4, (c % 4) * P:(c % 4 + 1) * P], k[:, d, h * P:(h + 1) * P],
                                      q[:, d, h * P:(h + 1) * P], start=True, stop=True)
                ins.then_inc(level_done, 1)

            for c in range(N_BVR):
                n = BVR + c
                if c == 0:
                    pe.wait_ge(qk_copied, 2 * B_HEADS)
                    pe.wait_ge(gcum_copied, 1)
                    level(0)
                if c == KB:
                    pe.wait_ge(bv_copied, 4)
                kb = c % KB
                moving_tile(n % 2, n + 1, 0, hT_hi[:, kb, :], hT_lo[:, kb, :], kb == 0, kb == KB - 1)
                if c % 2 == 1:
                    level(c // 2 + 1)
            pe.wait_ge(level_kept, B_LEVELS + 2)
            pe.wait_ge(silu_done, TT)
            for h in range(TT):
                for d in range(B_HEADS):
                    o = psum[:, 2 * h + d // 2, (d % 2) * B_HV:(d % 2 + 1) * B_HV]
                    if h == 1:
                        product(o, score_x[:, d, :], bv[:, 0, d * B_HV:(d + 1) * B_HV], start=True)
                    ins = product(o, score_in[:, TT * d + h, :], bv[:, h, d * B_HV:(d + 1) * B_HV], start=h == 0, stop=True)
                ins.then_inc(o_done, 1)
            for h in range(TT):
                pe.wait_ge(o_ready, h + 1)
                turn(bo[:, h, :], 4 + 2 * h, KB).then_inc(o_turned, 1)
            pe.wait_ge(oT_lo_ready, TT)
            for kb in range(KB):
                n = BOUT + kb
                moving_tile(n % 2, n + 1, 0, hT_hi[:, kb, :], hT_lo[:, kb, :], kb == 0, kb == KB - 1)
            peer(1)


def _layout(i):
    a = {k: np.asarray(v) for k, v in i.items()}

    def moving(w, blocks):
        kb = w.shape[0] // P
        return w.reshape(kb, P, blocks, TILE).transpose(2, 0, 1, 3).reshape(blocks * kb, P, TILE)

    def stationary(w):
        n = w.shape[1] // P
        return w.reshape(KB, P, n, P).transpose(2, 1, 0, 3).reshape(n, P, TILE)

    s, tk = np.arange(P)[:, None], np.arange(P)[None, :]
    masks = [((s ^ tk) >> j == 1) & (tk > s) for j in range(B_LEVELS)] + [s == tk]
    b_w = a["b_w_in"][0]
    v_first = np.concatenate([a["a_w_in"][0][:, A_WIDTH:], a["a_w_in"][0][:, :A_WIDTH]], axis=1)
    r = {
        "x": a["x"][0],
        "a_in": moving(v_first, A_BLOCKS),
        "a_out": moving(a["a_w_out"][0], 1),
        "b_in": np.concatenate([a["a_b_in"][0][A_WIDTH:], a["a_b_in"][0][:A_WIDTH]]),
        "ln_g": a["a_ln_g"][0],
        "ln_b": a["a_ln_b"][0],
        "w_sT": a["a_w_s"][0].transpose(2, 0, 1),
        "b_sT": a["a_b_s"][0].T,
        "gains": np.stack([a[k][l].reshape(KB, P).T for l in range(2) for k in ("norm_mix", "norm_ffn")], axis=1),
        "final_norm": a["final_norm"],
        "keysT": np.stack([np.stack([a[k][l].T for k in ("p_k1", "p_k2")], axis=1) for l in range(2)], axis=1),
        "b_qk": stationary(b_w[:, :2 * B_KEY]),
        "b_vr": moving(b_w[:, 2 * B_KEY:2 * B_KEY + 2 * D], 2),
        "w_g": b_w[:, 2 * B_KEY + 2 * D:].reshape(KB, P, B_RANK).transpose(1, 0, 2),
        "w_g2": a["b_w_g2"][0],
        "b_g": a["b_b_g"][0],
        "b_norm": a["b_norm"][0],
        "b_out": moving(a["b_w_out"][0], 1),
        "consts": np.stack([np.eye(P), np.broadcast_to(np.arange(P), (P, P)), (s <= tk) / 16.0], axis=1).astype(np.float32),
        "masks": np.stack(masks, axis=1).astype(np.uint32),
    }
    for l in range(2):
        r[f"w_q{l}"] = stationary(a["p_w_q"][l])
        r[f"u{l}"] = a["p_u"][l].reshape(NK, NK, KB, P).transpose(1, 3, 2, 0).reshape(NK, P, TILE)
        r[f"v{l}"] = a["p_v"][l].reshape(NK, NK, D).transpose(1, 0, 2)
    return {k: np.ascontiguousarray(v) for k, v in r.items()}


def kernel(**inputs):
    import concourse.bacc as bacc
    from concourse.bass_utils import run_bass_kernel_spmd

    arrays = _layout(inputs)
    nc = bacc.Bacc("TRN2", target_bir_lowering=False, num_devices=1)
    t = {k: nc.dram_tensor(f"in_{k}", v.shape, mybir.dt.from_np(v.dtype), kind="ExternalInput").ap() for k, v in arrays.items()}
    out = nc.dram_tensor("out_0", (TT, P, D), F32, kind="ExternalOutput").ap()
    trunk(nc, t, out)
    r = run_bass_kernel_spmd(nc, [{f"in_{k}": v for k, v in arrays.items()}], core_ids=[0])
    return r.results[0]["out_0"].reshape(1, T, D)
```

```python
from contextlib import ExitStack

import numpy as np

import concourse.bass as bass
from concourse import mybir

F32 = mybir.dt.float32
F32R = mybir.dt.float32r
BF16 = mybir.dt.bfloat16
U32 = mybir.dt.uint32
ALU = mybir.AluOpType
ACT = mybir.ActivationFunctionType
AX = mybir.AxisListType

P = 128
D = 1024
KB = D // P
T = 256
TT = T // P
TILE = 1024
BANK = 512
EPS = 1e-6

A_WIDTH = 2048
A_GROUPS = 8
A_GDIM = A_WIDTH // A_GROUPS
A_BLOCKS = 2 * A_WIDTH // TILE
YB = A_WIDTH // P

B_HEADS = 4
B_HK = 128
B_HV = 256
B_KEY = B_HEADS * B_HK
B_RANK = 16
B_LEVELS = 7

P_HEADS = 8
P_ROWS = 2 * P_HEADS
NK = 128
TOPK = 16
PICKS = P_HEADS * TOPK
N_SMALL = 6

GROUP = 4
GROUPS = T // GROUP
TURN_AT = 88
N_LATE = 2 * GROUPS // 4

RAW_SLOTS = 4
SPLIT_SLOTS = 2
LOWEST = -3.0e38

N_AIN = A_BLOCKS * KB
N_AOUT = YB
N_WQ = P_ROWS
N_EXP = NK
N_BQK = 2 * B_KEY // P
N_BVR = 2 * KB
N_BOUT = KB
AIN = 0
AOUT = AIN + N_AIN
WQ = [AOUT + N_AOUT, 0]
UT = [WQ[0] + N_WQ, 0]
VT = [UT[0] + N_EXP, 0]
BQK = VT[0] + N_EXP
BVR = BQK + N_BQK
BOUT = BVR + N_BVR
WQ[1] = BOUT + N_BOUT
UT[1] = WQ[1] + N_WQ
VT[1] = UT[1] + N_EXP
TILES = VT[1] + N_EXP


def lo_count(n):
    return n + 1 - N_LATE * sum(n >= VT[l] for l in range(2))


def trunk(nc, t, out):
    with ExitStack() as ctx:
        def sb(name, shape, dt=F32):
            return ctx.enter_context(nc.sbuf_tensor(name, shape, dt))

        def sem(name):
            return ctx.enter_context(nc.semaphore(name))

        raw = [sb(f"raw{s}", [P, TILE]) for s in range(RAW_SLOTS)]
        tile_hi = [sb(f"tile_hi{s}", [P, TILE], F32R) for s in range(SPLIT_SLOTS)]
        tile_lo = [sb(f"tile_lo{s}", [P, TILE], F32R) for s in range(SPLIT_SLOTS)]
        hT_hi = sb("hT_hi", [P, KB, T], F32R)
        hT_lo = sb("hT_lo", [P, KB, T], F32R)
        x = sb("x", [P, TT, D])
        consts = sb("consts", [P, 3, P])
        ident, iota, tri16 = consts[:, 0, :], consts[:, 1, :], consts[:, 2, :]
        keysT = sb("keysT", [P, 2, 2, NK])
        gains = sb("gains", [P, 4, KB])
        b_sT = sb("b_sT", [P, A_GROUPS])
        picks = sb("picks", [P, TT, 3, PICKS])
        picksT = sb("picksT", [P, 3, T])
        sumsq = sb("sumsq", [P, TT])
        meansq = sb("meansq", [P, TT])
        rms = sb("rms", [P, TT])
        rstd = sb("rstd", [P, TT])
        v_sum = sb("v_sum", [P, TT, 2])
        v_mean = sb("v_mean", [P, TT])
        head_sum = sb("head_sum", [P, TT, P_HEADS])
        head_inv = sb("head_inv", [P, TT, P_HEADS])

        def overlay(parts):
            with ExitStack() as own:
                return [own.enter_context(nc.sbuf_tensor(*p)) for p in parts]

        onehot1, onehot2 = overlay([("onehot1", [P, 2, GROUP, P], F32), ("onehot2", [P, 2, GROUP, P], F32)])
        (topv, topi, topi_f, candv, candpos, pos_a, pos_b, pos_af, pos_bf) = overlay([
            ("topv", [P, TT, P_ROWS, TOPK], F32),
            ("topi", [P, TT, P_ROWS, TOPK], U32),
            ("topi_f", [P, P_ROWS, TOPK], F32),
            ("candv", [P, P_HEADS, TOPK], F32),
            ("candpos", [P, P_HEADS, TOPK], U32),
            ("pos_a", [P, P_HEADS, TOPK], U32),
            ("pos_b", [P, P_HEADS, TOPK], U32),
            ("pos_af", [P, P_HEADS, TOPK], F32),
            ("pos_bf", [P, P_HEADS, TOPK], F32),
        ])
        sb("reserved_small", [P, 2048])
        equal2, gelu_out = overlay([("equal2", [P, 2, P, GROUP], BF16), ("gelu_out", [P, 2, T], F32)])
        w_hi0, w_hi1, w_lo0, w_lo1 = overlay([(f"w_{n}", [P, T], F32R) for n in ("hi0", "hi1", "lo0", "lo1")])
        w_hi, w_lo = [w_hi0, w_hi1], [w_lo0, w_lo1]
        sb("reserved_w", [P, 4 * T])
        numbers16 = sb("numbers16", [P, P, GROUP], BF16)
        picks16 = sb("picks16", [P, T], BF16)

        (acts,) = overlay([("acts", [P, NK, T], F32)])
        (_, qT, scores, cand, look) = overlay([
            ("pad_peer", [P, 80 * T], F32),
            ("qT", [P, P_ROWS, T], F32),
            ("scores", [P, TT, P_ROWS, NK], F32),
            ("cand", [P, P_HEADS, TOPK * TOPK], F32),
            ("look", [P, P_HEADS, TOPK, TOPK], F32),
        ])
        (b_in, ln_g, ln_b, zv, zu, wsT, yT_hi, yT_lo) = overlay([
            ("b_in", [P, 2 * A_WIDTH], F32),
            ("ln_g", [P, A_WIDTH], F32),
            ("ln_b", [P, A_WIDTH], F32),
            ("zv", [P, TT, A_WIDTH], F32),
            ("zu", [P, TT, A_WIDTH], F32),
            ("wsT", [P, A_GROUPS, P], F32),
            ("yT_hi", [P, YB, T], F32R),
            ("yT_lo", [P, YB, T], F32R),
        ])
        (gq, gk, gcum, z_la, z_tmp, ed0, ed1, qe0, qe1, ke0, ke1, score_in, score_x, bv, br, bsg, bo, bg_row,
         bnorm_row, w_g2, w_g, masks, g_lrT, head_ms) = overlay([
            ("gq", [P, B_HEADS, T], F32),
            ("gk", [P, B_HEADS, T], F32),
            ("gcum", [P, B_HEADS, T], F32),
            ("z_la", [P, TT, B_KEY], F32),
            ("z_tmp", [P, TT, B_KEY], F32),
            ("ed0", [P, B_HEADS, T], F32),
            ("ed1", [P, B_HEADS, T], F32),
            ("qe0", [P, B_HEADS, T], F32),
            ("qe1", [P, B_HEADS, T], F32),
            ("ke0", [P, B_HEADS, T], F32),
            ("ke1", [P, B_HEADS, T], F32),
            ("score_in", [P, B_HEADS * TT, P], F32),
            ("score_x", [P, B_HEADS, P], F32),
            ("bv", [P, TT, D], F32),
            ("br", [P, TT, D], F32),
            ("bsg", [P, TT, D], F32),
            ("bo", [P, TT, D], F32),
            ("bg_row", [P, B_KEY], F32),
            ("bnorm_row", [P, B_HV], F32),
            ("w_g2", [B_RANK, B_KEY], F32),
            ("w_g", [P, KB, B_RANK], F32),
            ("masks", [P, B_LEVELS + 1, P], U32),
            ("g_lrT", [B_RANK, T], F32),
            ("head_ms", [P, 4, TT * B_HEADS], F32),
        ])
        ed, qe, ke = [ed0, ed1], [qe0, qe1], [ke0, ke1]
        (_, hn, hT) = overlay([("pad_norm", [P, 112 * T], F32), ("hn", [P, TT, D], F32), ("hT", [P, KB, T], F32)])
        (_, final_row) = overlay([("pad_final", [P, 104 * T], F32), ("final_row", [P, D], F32)])

        psum = ctx.enter_context(nc.psum_tensor("psum", [P, 8, BANK], F32))

        raw_loaded = [sem(f"raw_loaded{s}") for s in range(RAW_SLOTS)]
        hi_ready, lo_ready, tile_used = sem("hi_ready"), sem("lo_ready"), sem("tile_used")
        numbers_ready = sem("numbers_ready")
        consts_loaded = sem("consts_loaded")
        x_loaded, small_loaded, gla_loaded, final_loaded = sem("x_loaded"), sem("small_loaded"), sem("gla_loaded"), sem("final_loaded")
        ws_masked = sem("ws_masked")
        dve_chain, act_chain = sem("dve_chain"), sem("act_chain")
        x_ready = [sem(f"x_ready{i}") for i in range(5)]
        squares = [sem(f"squares{i}") for i in range(5)]
        ms_ready = [sem(f"ms_ready{i}") for i in range(5)]
        rms_ready = [sem(f"rms_ready{i}") for i in range(5)]
        hn_ready = [sem(f"hn_ready{i}") for i in range(5)]
        hn_turned = [sem(f"hn_turned{i}") for i in range(4)]
        hT_ready = [sem(f"hT_ready{i}") for i in range(4)]
        hT_hi_ready = [sem(f"hT_hi_ready{i}") for i in range(4)]
        hT_lo_ready = [sem(f"hT_lo_ready{i}") for i in range(4)]
        ain_biased, ain_gelu = sem("ain_biased"), sem("ain_gelu")
        v_centred, v_squares, v_ms, v_std, v_normed = sem("v_centred"), sem("v_squares"), sem("v_ms"), sem("v_std"), sem("v_normed")
        sv_done, y_ready, y_turned, yT_hi_ready, yT_lo_ready = sem("sv_done"), sem("y_ready"), sem("y_turned"), sem("yT_hi_ready"), sem("yT_lo_ready")
        q_copied = [sem(f"q_copied{l}") for l in range(2)]
        scores_done = [sem(f"scores_done{l}") for l in range(2)]
        scores_copied = [sem(f"scores_copied{l}") for l in range(2)]
        gelu_done = [sem(f"gelu_done{l}") for l in range(2)]
        shifted = [sem(f"shifted{l}") for l in range(2)]
        exps = [sem(f"exps{l}") for l in range(2)]
        gates_ready = [sem(f"gates_ready{l}") for l in range(2)]
        picks_turned = [sem(f"picks_turned{l}") for l in range(2)]
        picksT_ready = [sem(f"picksT_ready{l}") for l in range(2)]
        ones_ready = [sem(f"ones_ready{l}") for l in range(2)]
        equal2_ready = [sem(f"equal2_ready{l}") for l in range(2)]
        onehot1_ready = [sem(f"onehot1_ready{l}") for l in range(2)]
        onehot2_ready = [sem(f"onehot2_ready{l}") for l in range(2)]
        late_lo_ready = [sem(f"late_lo_ready{l}") for l in range(2)]
        late_gated = [sem(f"late_gated{l}") for l in range(2)]
        gmat_done = [sem(f"gmat_done{l}") for l in range(2)]
        gated = [sem(f"gated{l}") for l in range(2)]
        w_hi_ready = [sem(f"w_hi_ready{l}") for l in range(2)]
        w_lo_ready = [sem(f"w_lo_ready{l}") for l in range(2)]
        glr_done, glr_copied, la_done, z_ready, la_abs, la_exp, la_ln, la_ready = (
            sem("glr_done"), sem("glr_copied"), sem("la_done"), sem("z_ready"), sem("la_abs"), sem("la_exp"), sem("la_ln"), sem("la_ready"))
        gcum_done, gcum_copied, qk_copied = sem("gcum_done"), sem("gcum_copied"), sem("qk_copied")
        score_zeroed, diff_ready, decay_ready, qk_decayed, level_done, level_kept = (
            sem("score_zeroed"), sem("diff_ready"), sem("decay_ready"), sem("qk_decayed"), sem("level_done"), sem("level_kept"))
        bv_copied, sig_done, silu_done, o_done, o_squares, o_ms, o_rms, o_ready, o_turned, oT_hi_ready, oT_lo_ready = (
            sem("bv_copied"), sem("sig_done"), sem("silu_done"), sem("o_done"), sem("o_squares"), sem("o_ms"), sem("o_rms"),
            sem("o_ready"), sem("o_turned"), sem("oT_hi_ready"), sem("oT_lo_ready"))
        normed_out, stored = sem("normed_out"), sem("stored")

        def bank_pair(b, n=2):
            return psum[:, b:b + n, :].rearrange("p b c -> p (b c)")

        block = ctx.enter_context(nc.Block())

        @block.sync
        def _(sp):
            sp.dma_start(x[:, :, :], t["x"].rearrange("(h p) d -> p h d", p=P)).then_inc(x_loaded, 16)
            sp.dma_start(consts[:, :, :], t["consts"]).then_inc(consts_loaded, 16)
            sp.dma_start(gains[:, :, :], t["gains"]).then_inc(consts_loaded, 16)

            def load(src, slot):
                sp.dma_start(raw[slot][:, :], src).then_inc(raw_loaded[slot], 16)

            def stage(name, first, start, end, made=lo_ready, offset=None):
                if offset is None:
                    offset = lo_count(first + start - RAW_SLOTS) - (start - RAW_SLOTS)
                with sp.Fori(start // RAW_SLOTS, end // RAW_SLOTS) as i:
                    for s in range(RAW_SLOTS):
                        sp.wait_ge(made, i * RAW_SLOTS + (offset + s - RAW_SLOTS))
                        load(t[name][i * RAW_SLOTS + s], s)

            for s in range(RAW_SLOTS):
                load(t["a_in"][s], s)
            stage("a_in", AIN, RAW_SLOTS, N_AIN)
            stage("a_out", AOUT, 0, N_AOUT)
            for l in range(2):
                stage(f"w_q{l}", WQ[l], 0, N_WQ)
                early = N_EXP - N_LATE
                stage(f"u{l}", UT[l], 0, early + RAW_SLOTS)
                stage(f"u{l}", UT[l], early + RAW_SLOTS, N_EXP, late_lo_ready[l], 1 - early)
                for s in range(RAW_SLOTS):
                    sp.wait_ge(late_lo_ready[l], N_LATE - RAW_SLOTS + s + 1)
                    load(t[f"v{l}"][s], s)
                stage(f"v{l}", VT[l], RAW_SLOTS, N_EXP)
                if l == 0:
                    stage("b_qk", BQK, 0, N_BQK)
                    stage("b_vr", BVR, 0, N_BVR)
                    stage("b_out", BOUT, 0, N_BOUT)
            for h in range(TT):
                sp.wait_ge(normed_out, h + 1)
                sp.dma_start(out[h], hn[:, h, :]).then_inc(stored, 16)
            sp.wait_ge(stored, 16 * TT)

        @block.gpsimd
        def _(pool):
            small = [(wsT[:, :, :], t["w_sT"]), (b_sT[:, :], t["b_sT"]),
                     (b_in[:, :], t["b_in"].partition_broadcast(P)),
                     (ln_g[:, :], t["ln_g"].partition_broadcast(P)), (ln_b[:, :], t["ln_b"].partition_broadcast(P)),
                     (keysT[:, :, :, :], t["keysT"])]
            for dst, src in small:
                pool.dma_start(dst, src).then_inc(small_loaded, 16)
            pool.wait_ge(small_loaded, 16 * N_SMALL)
            pool.affine_select(out=wsT[:, :, :], in_=wsT[:, :, :], compare_op=ALU.is_ge, fill=0.0, base=0,
                               pattern=[[0, A_GROUPS], [1, P]], channel_multiplier=-1).then_inc(ws_masked, 1)

            def late_experts(l):
                pool.wait_ge(shifted[l], TT)
                pool.memset(acts[:, N_EXP - N_LATE:N_EXP, :], 1.0).then_inc(ones_ready[l], 1)
                first = UT[l] + N_EXP - N_LATE
                with pool.Fori(0, N_LATE // RAW_SLOTS) as i:
                    for c in range(RAW_SLOTS):
                        pool.wait_ge(hi_ready, i * RAW_SLOTS + (first + c + 1))
                        pool.tensor_tensor(tile_lo[c % SPLIT_SLOTS][:, :], raw[c][:, :], tile_hi[c % SPLIT_SLOTS][:, :].bitcast(F32),
                                           ALU.subtract).then_inc(late_lo_ready[l], 1)

            late_experts(0)
            pool.wait_ge(x_ready[2], 4)
            gla = [(masks[:, :, :], t["masks"]), (w_g[:, :, :], t["w_g"]), (w_g2[:, :], t["w_g2"]),
                   (bg_row[:, :], t["b_g"].partition_broadcast(P)), (bnorm_row[:, :], t["b_norm"].partition_broadcast(P))]
            for dst, src in gla:
                pool.dma_start(dst, src).then_inc(gla_loaded, 16)
            pool.memset(score_in[:, :, :], 0.0).then_inc(score_zeroed, 1)
            late_experts(1)
            pool.wait_ge(x_ready[4], 4)
            pool.dma_start(final_row[:, :], t["final_norm"].partition_broadcast(P)).then_inc(final_loaded, 16)

        @block.scalar
        def _(act):
            def hi(slot, raw_count, used):
                act.wait_ge(raw_loaded[slot], raw_count)
                if used is not None:
                    act.wait_ge(tile_used, used)
                act.activation(tile_hi[slot % SPLIT_SLOTS][:, :], raw[slot][:, :], ACT.Copy).then_inc(hi_ready, 1)

            def hi_at(n):
                hi(n % RAW_SLOTS, 16 * (n // RAW_SLOTS + 1), n - 1 if n >= SPLIT_SLOTS else None)

            def hi_in(i, c, first):
                n = first + c
                hi(n % RAW_SLOTS, i * 16 + 16 * (n // RAW_SLOTS + 1), i * RAW_SLOTS + (n - 1))

            chained = [0]

            def norm(i):
                for h in range(TT):
                    if i == 0:
                        act.wait_ge(x_loaded, 16)
                    else:
                        act.wait_ge(x_ready[i], 2 * h + 2)
                    act.activation(hn[:, h, :], x[:, h, :], ACT.Square, accum_out=sumsq[:, h:h + 1]).then_inc(squares[i], 1)
                if i == 0:
                    hi_at(0)
                    hi_at(1)
                for h in range(TT):
                    act.wait_ge(ms_ready[i], h + 1)
                    act.activation(rms[:, h:h + 1], meansq[:, h:h + 1], ACT.Sqrt).then_inc(rms_ready[i], 1)
                if i == 4:
                    return
                for h in range(TT):
                    act.wait_ge(hT_ready[i], h + 1)
                    act.activation(hT_hi[:, :, h * P:(h + 1) * P], hT[:, :, h * P:(h + 1) * P], ACT.Copy).then_inc(hT_hi_ready[i], 1)

            norm(0)

            def a_gelu(j):
                for h in range(TT):
                    act.wait_ge(ain_biased, 2 * TT * j + 2 * h + 2)
                    if j < 2:
                        z = zv[:, h, j * TILE:(j + 1) * TILE]
                        act.activation(z, z, ACT.Gelu, accum_out=v_sum[:, h, j:j + 1]).then_inc(ain_gelu, 1)
                    else:
                        z = zu[:, h, (j - 2) * TILE:(j - 1) * TILE]
                        act.activation(z, z, ACT.Gelu).then_inc(ain_gelu, 1)

            for n in range(2, AOUT + 2):
                hi_at(n)
                j = (n - 2) // KB - 1
                if (n - 2) % KB == 0 and 0 <= j < 3:
                    a_gelu(j)
                if n in (2 * KB + 4, 2 * KB + 5):
                    h = n - 2 * KB - 4
                    act.wait_ge(v_centred, h + 1)
                    act.activation(yT_hi[:, 8 * h:8 * h + 8, :].rearrange("p a b -> p (a b)"), zv[:, h, :],
                                   ACT.Square, accum_out=sumsq[:, h:h + 1]).then_inc(v_squares, 1)
                if n == 2 * KB + 7:
                    act.wait_ge(v_ms, 1)
                    act.activation(rms[:, :], meansq[:, :], ACT.Sqrt).then_inc(v_std, 1)
            a_gelu(3)
            for h in range(TT):
                act.wait_ge(y_turned, h + 1)
                for c in range(4):
                    act.activation(yT_hi[:, 4 * c:4 * c + 4, h * P:(h + 1) * P],
                                   psum[:, 4 * h + c, :].rearrange("p (a b) -> p a b", a=4), ACT.Copy).then_inc(yT_hi_ready, 1)
            for n in range(AOUT + 2, WQ[0] + 2):
                hi_at(n)

            def peer(l):
                norm(1 + 2 * l)
                with act.Fori(0, N_WQ // RAW_SLOTS) as i:
                    for c in range(RAW_SLOTS):
                        hi_in(i, c, WQ[l] + 2)
                        act.wait_ge(tile_used, i * RAW_SLOTS + (WQ[l] + c + 1))
                        act.activation(qT[:, i * RAW_SLOTS + c, :], psum[:, c, 0:T], ACT.Copy).then_inc(q_copied[l], 1)
                for h in range(TT):
                    for c in range(4):
                        act.wait_ge(scores_done[l], 4 * h + c + 1)
                        act.activation(scores[:, h, 4 * c:4 * c + 4, :].rearrange("p a b -> p (a b)"), psum[:, 4 * h + c, :],
                                       ACT.Copy).then_inc(scores_copied[l], 1)

                def expert_acts(first, last):
                    with act.Fori(first // RAW_SLOTS, last // RAW_SLOTS) as i:
                        for c in range(RAW_SLOTS):
                            hi_in(i, c, UT[l] + 2)
                            act.wait_ge(tile_used, i * RAW_SLOTS + (UT[l] + c + 1))
                            act.activation(acts[:, i * RAW_SLOTS + c, :], psum[:, c, 0:T], ACT.Gelu).then_inc(gelu_done[l], 1)

                act.preload_act_table(ACT.Gelu)
                expert_acts(0, 76)
                for h in range(TT):
                    act.wait_ge(shifted[l], h + 1)
                    act.activation(picks[:, h, 2, :], picks[:, h, 2, :], ACT.Exp).then_inc(exps[l], 1)
                act.preload_act_table(ACT.Gelu)
                expert_acts(76, TURN_AT)
                act.wait_ge(picks_turned[l], 1)
                act.activation(picksT[:, 0:2, :].rearrange("p a b -> p (a b)"), psum[:, 4, :], ACT.Copy).then_inc(picksT_ready[l], 1)
                act.activation(picksT[:, 2, :], psum[:, 5, 0:T], ACT.Copy).then_inc(picksT_ready[l], 1)
                expert_acts(TURN_AT, N_EXP - N_LATE)

                def gated_onehots(token0, slot, ready, used):
                    act.wait_ge(equal2_ready[l], ready)
                    if used is not None:
                        act.wait_ge(gmat_done[l], used)
                    for c in range(GROUP):
                        ins = act.activation(onehot2[:, slot, c, :], equal2[:, slot, :, c], ACT.Copy,
                                             scale=picksT[:, 2, bass.ds(token0 + c, 1)])
                    ins.then_inc(onehot2_ready[l], 1)

                def late_tile(i, c, more):
                    k = N_EXP - N_LATE + c
                    act.wait_ge(tile_used, i * RAW_SLOTS + (UT[l] + k + 1))
                    if c >= SPLIT_SLOTS or not (isinstance(i, int) and i == 0):
                        act.wait_ge(late_gated[l], i * RAW_SLOTS + (c - 1))
                    act.activation(gelu_out[:, c % 2, :], psum[:, c, 0:T], ACT.Gelu).then_inc(gelu_done[l], 1)
                    hi_in(i, c, UT[l] + 2 + N_EXP - N_LATE)
                    if more:
                        for b in range(2):
                            g = 2 * c + b + 4
                            gated_onehots(i * (8 * GROUP) + g * GROUP, b, i * 8 + (g + 1), i * 8 + (g - 1))

                act.wait_ge(picksT_ready[l], 2)
                for g in range(4):
                    gated_onehots(g * GROUP, g % 2, g + 1, g - 1 if g >= 2 else None)
                for c in range(RAW_SLOTS):
                    late_tile(0, c, True)
                with act.Fori(1, N_LATE // RAW_SLOTS - 1) as i:
                    for c in range(RAW_SLOTS):
                        late_tile(i, c, True)
                for c in range(RAW_SLOTS):
                    late_tile(N_LATE // RAW_SLOTS - 1, c, c < 2)

                def gated_hi(k, slot, used):
                    if used is not None:
                        act.wait_ge(tile_used, used)
                    act.activation(w_hi[slot][:, :], acts[:, k, :], ACT.Copy).then_inc(w_hi_ready[l], 1)

                act.wait_ge(gated[l], GROUPS)
                act.wait_ge(late_gated[l], N_LATE)
                gated_hi(0, 0, None)
                gated_hi(1, 1, None)
                with act.Fori(0, N_EXP // RAW_SLOTS - 1) as i:
                    for c in range(RAW_SLOTS):
                        gated_hi(i * RAW_SLOTS + (c + 2), c % 2, i * RAW_SLOTS + (VT[l] + c + 1))
                        hi_in(i, c, VT[l] + 2)
                for k in (N_EXP - 2, N_EXP - 1):
                    gated_hi(k, k % 2, VT[l] + k - 1)
                    hi_at(VT[l] + k)

            peer(0)
            hi_at(BQK)
            hi_at(BQK + 1)
            norm(2)
            act.wait_ge(glr_done, 1)
            act.activation(g_lrT[:, :], psum[0:B_RANK, 4, 0:T], ACT.Copy).then_inc(glr_copied, 1)
            for n in range(BQK + 2, BVR + 2):
                hi_at(n)
                c = n - 2 - BQK
                act.wait_ge(tile_used, BQK + c + 1)
                if c < B_HEADS:
                    act.activation(gq[:, c, :], psum[:, c % 4, 0:T], ACT.Copy, scale=float(B_HK) ** -0.5).then_inc(qk_copied, 1)
                else:
                    act.activation(gk[:, c - B_HEADS, :], psum[:, c % 4, 0:T], ACT.Copy).then_inc(qk_copied, 1)
                if c == 1:
                    act.wait_ge(z_ready, 1)
                    act.activation(z_tmp[:, :, :], z_la[:, :, :], ACT.Abs).then_inc(la_abs, 1)
                    act.wait_ge(la_abs, 1)
                    act.activation(z_tmp[:, :, :], z_tmp[:, :, :], ACT.Exp, scale=-1.0).then_inc(la_exp, 1)
                    act.wait_ge(la_exp, 1)
                    act.activation(z_tmp[:, :, :], z_tmp[:, :, :], ACT.Ln, bias=1.0).then_inc(la_ln, 1)
            act.wait_ge(gcum_done, 1)
            act.activation(gcum[:, :, :].rearrange("p a b -> p (a b)"), bank_pair(5), ACT.Copy).then_inc(gcum_copied, 1)

            def decay(L):
                act.wait_ge(diff_ready, L)
                act.activation(ed[L % 2][:, :, :], ed[L % 2][:, :, :], ACT.Exp).then_inc(decay_ready, 1)

            decay(1)
            for n in range(BVR + 2, BOUT + 2):
                hi_at(n)
                c = n - 2 - BVR
                if c % 2 == 0 and c // 2 + 2 <= B_LEVELS + 1:
                    decay(c // 2 + 2)
                if c == KB - 1:
                    for b in range(4):
                        act.wait_ge(tile_used, BVR + KB)
                        act.activation(bv[:, b // 2, (b % 2) * BANK:(b % 2 + 1) * BANK], psum[:, b, :], ACT.Copy).then_inc(bv_copied, 1)
            for h in range(TT):
                act.wait_ge(tile_used, BOUT)
                act.activation(bsg[:, h, :], bank_pair(2 * h), ACT.Sigmoid).then_inc(sig_done, 1)
            for h in range(TT):
                act.wait_ge(o_done, h + 1)
                act.activation(bo[:, h, :], bank_pair(2 * h), ACT.Square).then_inc(o_squares, 1)
            act.wait_ge(o_ms, 1)
            act.activation(head_ms[:, 2, :], head_ms[:, 1, :], ACT.Sqrt).then_inc(o_rms, 1)
            for h in range(TT):
                act.wait_ge(o_turned, h + 1)
                act.activation(hT_hi[:, :, h * P:(h + 1) * P], bank_pair(4 + 2 * h).rearrange("p (a b) -> p a b", a=KB),
                               ACT.Copy).then_inc(oT_hi_ready, 1)
            for n in range(BOUT + 2, WQ[1] + 2):
                hi_at(n)
            peer(1)
            norm(4)

        @block.vector
        def _(dve):
            def lo(slot, ready):
                dve.wait_ge(hi_ready, ready)
                s = slot % SPLIT_SLOTS
                dve.tensor_tensor(tile_lo[s][:, :], raw[slot][:, :], tile_hi[s][:, :].bitcast(F32),
                                  ALU.subtract).then_inc(lo_ready, 1)

            def lo_at(n):
                lo(n % RAW_SLOTS, n + 1)

            def lo_in(i, c, first):
                lo((first + c) % RAW_SLOTS, i * RAW_SLOTS + (first + c + 1))

            chain = [0]

            def did(ins):
                ins.then_inc(dve_chain, 1)
                chain[0] += 1
                return chain[0]

            def after(number):
                dve.wait_ge(dve_chain, number)

            def norm(i):
                for h in range(TT):
                    dve.wait_ge(squares[i], h + 1)
                    dve.tensor_scalar(meansq[:, h:h + 1], sumsq[:, h:h + 1], 1.0 / D, EPS, ALU.mult, ALU.add).then_inc(ms_ready[i], 1)
                for h in range(TT):
                    dve.wait_ge(rms_ready[i], h + 1)
                    after(did(dve.reciprocal(rstd[:, h:h + 1], rms[:, h:h + 1])))
                    dve.tensor_scalar(hn[:, h, :], x[:, h, :], rstd[:, h:h + 1], None, ALU.mult).then_inc(hn_ready[i], 1)
                    if i == 4:
                        dve.wait_ge(hn_ready[4], h + 1)
                        dve.wait_ge(final_loaded, 16)
                        dve.tensor_tensor(hn[:, h, :], hn[:, h, :], final_row[:, :], ALU.mult).then_inc(normed_out, 1)
                if i == 4:
                    return
                if i == 0:
                    lo_at(0)
                    lo_at(1)
                for h in range(TT):
                    dve.wait_ge(hn_turned[i], h + 1)
                    cols = slice(h * P, (h + 1) * P)
                    dve.tensor_tensor(hT[:, :, cols], bank_pair(2 * h).rearrange("p (a b) -> p a b", a=KB),
                                      gains[:, i, :].unsqueeze(2).broadcast_to([P, KB, P]), ALU.mult).then_inc(hT_ready[i], 1)
                for h in range(TT):
                    dve.wait_ge(hT_hi_ready[i], h + 1)
                    cols = slice(h * P, (h + 1) * P)
                    dve.tensor_tensor(hT_lo[:, :, cols], hT[:, :, cols], hT_hi[:, :, cols].bitcast(F32),
                                      ALU.subtract).then_inc(hT_lo_ready[i], 1)

            def add_to_x(i, first_bank, last_tile):
                dve.wait_ge(tile_used, last_tile + 1)
                for b in range(4):
                    part = x[:, b // 2, (b % 2) * BANK:(b % 2 + 1) * BANK]
                    dve.tensor_tensor(part, psum[:, first_bank + b, :], part, ALU.add).then_inc(x_ready[i], 1)

            dve.wait_ge(x_loaded, 16)
            dve.wait_ge(consts_loaded, 16 * 2)
            norm(0)
            dve.tensor_copy(numbers16[:, :, :], iota.unsqueeze(2).broadcast_to([P, P, GROUP])).then_inc(numbers_ready, 1)
            dve.wait_ge(small_loaded, 16 * N_SMALL)

            def a_bias(j):
                dve.wait_ge(tile_used, (j + 1) * KB)
                for b in range(4):
                    h, cols = b // 2, (j % 2) * TILE + (b % 2) * BANK
                    z = zv if j < 2 else zu
                    dve.tensor_tensor(z[:, h, cols:cols + BANK], psum[:, 4 * (j % 2) + b, :],
                                      b_in[:, j * TILE + (b % 2) * BANK:j * TILE + (b % 2 + 1) * BANK], ALU.add).then_inc(ain_biased, 1)

            for n in range(2, AOUT + 2):
                lo_at(n)
                if (n - 1) % KB == 0 and n > KB:
                    a_bias((n - 1) // KB - 1)
                step = n - 2 * KB
                if step == 3:
                    dve.wait_ge(ain_gelu, 4)
                    after(did(dve.tensor_tensor(v_mean[:, :], v_sum[:, :, 0], v_sum[:, :, 1], ALU.add)))
                    after(did(dve.tensor_scalar(v_mean[:, :], v_mean[:, :], 1.0 / A_WIDTH, None, ALU.mult)))
                    for h in range(TT):
                        dve.tensor_scalar(zv[:, h, :], zv[:, h, :], v_mean[:, h:h + 1], None, ALU.subtract).then_inc(v_centred, 1)
                if step == 6:
                    dve.wait_ge(v_squares, TT)
                    dve.tensor_scalar(meansq[:, :], sumsq[:, :], 1.0 / A_WIDTH, EPS, ALU.mult, ALU.add).then_inc(v_ms, 1)
                if step == 8:
                    dve.wait_ge(v_std, 1)
                    after(did(dve.reciprocal(rstd[:, :], rms[:, :])))
                if step in (10, 12):
                    h = (step - 10) // 2
                    normed_v = did(dve.scalar_tensor_tensor(zv[:, h, :], zv[:, h, :], rstd[:, h:h + 1], ln_g[:, :], ALU.mult, ALU.mult))
                if step in (11, 13):
                    h = (step - 11) // 2
                    after(normed_v)
                    dve.tensor_tensor(zv[:, h, :], zv[:, h, :], ln_b[:, :], ALU.add).then_inc(v_normed, 1)
            dve.wait_ge(ain_gelu, 8)
            for h in range(TT):
                dve.wait_ge(sv_done, h + 1)
                for g in range(A_GROUPS):
                    u = zu[:, h, g * A_GDIM:(g + 1) * A_GDIM]
                    bank, col = 4 * h + g // 2, (g % 2) * A_GDIM
                    dve.scalar_tensor_tensor(u, psum[:, bank, col:col + A_GDIM], b_sT[:, g:g + 1], u,
                                             ALU.add, ALU.mult).then_inc(y_ready, 1)
            for h in range(TT):
                for c in range(4):
                    dve.wait_ge(yT_hi_ready, 4 * h + c + 1)
                    dst = (slice(None), slice(4 * c, 4 * c + 4), slice(h * P, (h + 1) * P))
                    dve.tensor_tensor(yT_lo[dst], psum[:, 4 * h + c, :].rearrange("p (a b) -> p a b", a=4),
                                      yT_hi[dst].bitcast(F32), ALU.subtract).then_inc(yT_lo_ready, 1)
            for n in range(AOUT + 2, WQ[0] + 2):
                lo_at(n)
            add_to_x(1, 0, WQ[0] - 1)

            def top16(rows, values, places, between):
                n8 = [did(dve.max(values[r][:, 0:8], rows[r])) for r in range(2)]
                for r in range(2):
                    after(n8[r])
                    n8[r] = did(dve.max_index(places[r][:, 0:8], values[r][:, 0:8], rows[r]))
                if between:
                    between[0]()
                for r in range(2):
                    after(n8[r])
                    n8[r] = did(dve.match_replace(rows[r], values[r][:, 0:8], rows[r], LOWEST))
                for r in range(2):
                    after(n8[r])
                    n8[r] = did(dve.max(values[r][:, 8:16], rows[r]))
                if len(between) > 1:
                    between[1]()
                for r in range(2):
                    after(n8[r])
                    n8[r] = did(dve.max_index(places[r][:, 8:16], values[r][:, 8:16], rows[r]))
                return n8[1]

            def peer(l):
                norm(1 + 2 * l)
                with dve.Fori(0, N_WQ // RAW_SLOTS) as i:
                    for c in range(RAW_SLOTS):
                        lo_in(i, c, WQ[l] + 2)
                n = UT[l] + 2
                dve.wait_ge(scores_copied[l], 4 * TT)
                for h in range(TT):
                    for r in range(0, P_ROWS, 2):
                        lo_at(n)
                        top16([scores[:, h, r + k, :] for k in range(2)], [topv[:, h, r + k, :] for k in range(2)],
                              [topi[:, h, r + k, :] for k in range(2)], [lambda: lo_at(n + 1)])
                        n += 2
                for h in range(TT):
                    lo_at(n)
                    n += 1
                    after(chain[0])
                    v1 = topv[:, h, 0:P_ROWS:2, :].unsqueeze(3).broadcast_to([P, P_HEADS, TOPK, TOPK])
                    v2 = topv[:, h, 1:P_ROWS:2, :].unsqueeze(2).broadcast_to([P, P_HEADS, TOPK, TOPK])
                    sums = did(dve.tensor_tensor(cand[:, :, :].rearrange("p g (a b) -> p g a b", a=TOPK), v1, v2, ALU.add))
                    after(sums)
                    for g in range(0, P_HEADS, 2):
                        lo_at(n)
                        top16([cand[:, g + k, :] for k in range(2)], [candv[:, g + k, :] for k in range(2)],
                              [candpos[:, g + k, :] for k in range(2)], [lambda: lo_at(n + 1), lambda: lo_at(n + 2)])
                        n += 3
                    lo_at(n)
                    n += 1
                    after(chain[0])
                    a1 = did(dve.tensor_scalar(pos_a[:, :, :], candpos[:, :, :], 4, None, ALU.logical_shift_right))
                    a2 = did(dve.tensor_scalar(pos_b[:, :, :], candpos[:, :, :], 15, None, ALU.bitwise_and))
                    a3 = did(dve.tensor_copy(topi_f[:, :, :], topi[:, h, :, :]))
                    after(a1)
                    a1 = did(dve.tensor_copy(pos_af[:, :, :], pos_a[:, :, :]))
                    after(a2)
                    a2 = did(dve.tensor_copy(pos_bf[:, :, :], pos_b[:, :, :]))
                    after(a3)
                    for half, pos in ((0, pos_af), (1, pos_bf)):
                        after((a1, a2)[half])
                        lo_at(n)
                        want = pos[:, :, :].unsqueeze(3).broadcast_to([P, P_HEADS, TOPK, TOPK])
                        ranks = iota[:, 0:TOPK].unsqueeze(1).unsqueeze(1).broadcast_to([P, P_HEADS, TOPK, TOPK])
                        numbers = topi_f[:, half:P_ROWS:2, :].unsqueeze(2).broadcast_to([P, P_HEADS, TOPK, TOPK])
                        eq = did(dve.tensor_tensor(look[:, :, :, :], want, ranks, ALU.is_equal))
                        lo_at(n + 1)
                        after(eq)
                        eq = did(dve.tensor_tensor(look[:, :, :, :], look[:, :, :, :], numbers, ALU.mult))
                        lo_at(n + 2)
                        after(eq)
                        eq = did(dve.tensor_reduce(picks[:, h, half, :].rearrange("p (g k) -> p g k", g=P_HEADS),
                                                   look[:, :, :, :], AX.X, ALU.add))
                        after(eq)
                        n += 3
                    dve.tensor_tensor(picks[:, h, 2, :].rearrange("p (g k) -> p g k", g=P_HEADS), candv[:, :, :],
                                      candv[:, :, 0:1].broadcast_to([P, P_HEADS, TOPK]), ALU.subtract).then_inc(shifted[l], 1)
                    dve.wait_ge(shifted[l], h + 1)
                while n < UT[l] + 2 + 80:
                    lo_at(n)
                    n += 1
                for h in range(TT):
                    e = picks[:, h, 2, :].rearrange("p (g k) -> p g k", g=P_HEADS)
                    dve.wait_ge(exps[l], h + 1)
                    after(did(dve.tensor_reduce(head_sum[:, h, :], e, AX.X, ALU.add)))
                    after(did(dve.reciprocal(head_inv[:, h, :], head_sum[:, h, :])))
                    dve.tensor_tensor(e, e, head_inv[:, h, :].unsqueeze(2).broadcast_to([P, P_HEADS, TOPK]),
                                      ALU.mult).then_inc(gates_ready[l], 1)
                early = N_EXP - N_LATE - 2
                with dve.Fori(0, (early - 80) // RAW_SLOTS) as i:
                    for c in range(RAW_SLOTS):
                        lo_in(i, c, UT[l] + 2 + 80)
                for k in range(early - early % RAW_SLOTS, early):
                    lo_at(UT[l] + 2 + k)

                def onehot(token0, slot):
                    rows = iota.unsqueeze(1).broadcast_to([P, GROUP, P])
                    number = picksT[:, 0, bass.ds(token0, GROUP)].unsqueeze(2).broadcast_to([P, GROUP, P])
                    dve.tensor_tensor(onehot1[:, slot, :, :], rows, number, ALU.is_equal).then_inc(onehot1_ready[l], 1)

                def gate(token0, c, done):
                    dve.wait_ge(gmat_done[l], done)
                    a = acts[:, :, bass.ds(token0, GROUP)].rearrange("p i t -> p t i")
                    dve.tensor_tensor(a, psum[:, 4 + c % 4, :].rearrange("p (t i) -> p t i", t=GROUP), a, ALU.mult).then_inc(gated[l], 1)

                def equal(token0, slot, read):
                    if read is not None:
                        dve.wait_ge(onehot2_ready[l], read)
                    number = picks16[:, bass.ds(token0, GROUP)].unsqueeze(1).broadcast_to([P, P, GROUP])
                    dve.tensor_tensor(equal2[:, slot, :, :], numbers16[:, :, :], number, ALU.is_equal).then_inc(equal2_ready[l], 1)

                def late_tile(i, c):
                    last = isinstance(i, int)
                    for b in range(2):
                        g = 2 * c + b
                        gate(i * (8 * GROUP) + g * GROUP, g, i * 8 + (g + 1))
                        if not (last and g + 2 >= 8):
                            onehot(i * (8 * GROUP) + (g + 2) * GROUP, b)
                    for b in range(2):
                        g = 2 * c + b
                        if not (last and g + 4 >= 8):
                            equal(i * (8 * GROUP) + (g + 4) * GROUP, b, i * 8 + (g + 3))
                    dve.wait_ge(gelu_done[l], i * RAW_SLOTS + (N_EXP - N_LATE + c + 1))
                    dve.wait_ge(gated[l], i * 8 + (2 * c + 2))
                    place = acts[:, i * RAW_SLOTS + (N_EXP - N_LATE + c), :]
                    dve.tensor_tensor(place, place, gelu_out[:, c % 2, :], ALU.mult).then_inc(late_gated[l], 1)
                    dve.wait_ge(late_gated[l], i * RAW_SLOTS + (c + 1))

                dve.wait_ge(picksT_ready[l], 2)
                turned = did(dve.tensor_copy(picks16[:, :], picksT[:, 1, :]))
                onehot(0, 0)
                onehot(GROUP, 1)
                after(turned)
                dve.wait_ge(numbers_ready, 1)
                for g in range(4):
                    equal(g * GROUP, g % 2, g - 1 if g >= 2 else None)
                dve.wait_ge(ones_ready[l], 1)
                dve.wait_ge(gelu_done[l], N_EXP - N_LATE)
                with dve.Fori(0, N_LATE // RAW_SLOTS - 1) as i:
                    for c in range(RAW_SLOTS):
                        late_tile(i, c)
                for c in range(RAW_SLOTS):
                    late_tile(N_LATE // RAW_SLOTS - 1, c)
                lo_at(VT[l])
                lo_at(VT[l] + 1)

                def gated_lo(k, slot, ready):
                    dve.wait_ge(w_hi_ready[l], ready)
                    dve.tensor_tensor(w_lo[slot][:, :], acts[:, k, :], w_hi[slot][:, :].bitcast(F32), ALU.subtract).then_inc(w_lo_ready[l], 1)

                dve.wait_ge(gated[l], GROUPS)
                dve.wait_ge(late_gated[l], N_LATE)
                gated_lo(0, 0, 1)
                gated_lo(1, 1, 2)
                with dve.Fori(0, N_EXP // RAW_SLOTS - 1) as i:
                    for c in range(RAW_SLOTS):
                        gated_lo(i * RAW_SLOTS + (c + 2), c % 2, i * RAW_SLOTS + (c + 3))
                        lo_in(i, c, VT[l] + 2)
                for k in (N_EXP - 2, N_EXP - 1):
                    gated_lo(k, k % 2, k + 1)
                    lo_at(VT[l] + k)

            peer(0)
            lo_at(BQK)
            lo_at(BQK + 1)
            add_to_x(2, 4, BQK - 1)
            norm(2)
            for n in range(BQK + 2, BVR + 2):
                lo_at(n)
                c = n - 2 - BQK
                if c == 0:
                    dve.wait_ge(la_done, TT)
                    dve.wait_ge(gla_loaded, 16 * 5)
                    dve.tensor_tensor(z_la[:, :, :], psum[:, 5:7, :], bg_row[:, :].unsqueeze(1).broadcast_to([P, TT, B_KEY]),
                                      ALU.add).then_inc(z_ready, 1)
                if c == 2:
                    dve.wait_ge(la_ln, 1)
                    dve.scalar_tensor_tensor(z_la[:, :, :].rearrange("p a b -> p (a b)"), z_la[:, :, :].rearrange("p a b -> p (a b)"), 0.0,
                                             z_tmp[:, :, :].rearrange("p a b -> p (a b)"), ALU.min, ALU.subtract).then_inc(la_ready, 1)

            def diff(L):
                e, flat = ed[L % 2], gcum
                if L == 1:
                    last = gcum[:, :, P - 1:P].broadcast_to([P, B_HEADS, P])
                    dve.tensor_tensor(e[:, :, 0:P], last, gcum[:, :, 0:P], ALU.subtract)
                    dve.tensor_copy(e[:, :, P:T], gcum[:, :, P:T]).then_inc(diff_ready, 1)
                    return
                m = 1 << (L - 2)
                g4 = gcum[:, :, :].rearrange("p h (b w m) -> p (h b) w m", w=2, m=m)
                e4 = e[:, :, :].rearrange("p h (b w m) -> p (h b) w m", w=2, m=m)
                ref = g4[:, :, 0, m - 1:m].broadcast_to([P, B_HEADS * T // (2 * m), m])
                dve.tensor_tensor(e4[:, :, 0, :], ref, g4[:, :, 0, :], ALU.subtract)
                dve.tensor_tensor(e4[:, :, 1, :], g4[:, :, 1, :], ref, ALU.subtract).then_inc(diff_ready, 1)

            def decayed(L):
                if L == 0:
                    dve.wait_ge(qk_copied, 2 * B_HEADS)
                    return
                dve.wait_ge(decay_ready, L)
                if L >= 3:
                    dve.wait_ge(level_done, L - 1)
                dve.tensor_tensor(qe[L % 2][:, :, :], gq[:, :, :], ed[L % 2][:, :, :], ALU.mult)
                dve.tensor_tensor(ke[L % 2][:, :, :], gk[:, :, :], ed[L % 2][:, :, :], ALU.mult).then_inc(qk_decayed, 1)

            def keep(L):
                dve.wait_ge(level_done, L + 1)
                if L == 1:
                    dve.tensor_copy(score_x[:, :, :].rearrange("p a b -> p (a b)"), psum[:, 6, :]).then_inc(level_kept, 1)
                    return
                mask = masks[:, B_LEVELS if L == 0 else L - 2, :].unsqueeze(1).broadcast_to([P, B_HEADS * TT, P])
                dve.copy_predicated(score_in[:, :, :], mask,
                                    bank_pair(4 + 2 * (L % 2)).rearrange("p (a b) -> p a b", b=P)).then_inc(level_kept, 1)

            dve.wait_ge(gcum_copied, 1)
            decayed(0)
            diff(1)
            dve.wait_ge(score_zeroed, 1)
            levels = B_LEVELS + 2
            for n in range(BVR + 2, BOUT + 2):
                lo_at(n)
                c = n - 2 - BVR
                if c % 2 == 0:
                    if c // 2 + 2 < levels:
                        if c // 2 >= 1:
                            dve.wait_ge(qk_decayed, c // 2)
                        diff(c // 2 + 2)
                    decayed(c // 2 + 1)
                else:
                    if c > 1:
                        dve.wait_ge(level_kept, c // 2)
                    keep(c // 2)
            dve.wait_ge(level_kept, levels - 1)
            keep(levels - 1)
            for h in range(TT):
                dve.wait_ge(sig_done, h + 1)
                dve.tensor_tensor(br[:, h, :], bank_pair(2 * h), bsg[:, h, :], ALU.mult).then_inc(silu_done, 1)
            for h in range(TT):
                dve.wait_ge(o_squares, h + 1)
                last = did(dve.tensor_reduce(head_ms[:, 0, B_HEADS * h:B_HEADS * (h + 1)],
                                             bo[:, h, :].rearrange("p (g v) -> p g v", g=B_HEADS), AX.X, ALU.add))
            after(last)
            dve.tensor_scalar(head_ms[:, 1, :], head_ms[:, 0, :], 1.0 / B_HV, EPS, ALU.mult, ALU.add).then_inc(o_ms, 1)
            dve.wait_ge(o_rms, 1)
            after(did(dve.reciprocal(head_ms[:, 3, :], head_ms[:, 2, :])))
            for h in range(TT):
                o3 = bo[:, h, :].rearrange("p (g v) -> p g v", g=B_HEADS)
                inv = head_ms[:, 3, B_HEADS * h:B_HEADS * (h + 1)].unsqueeze(2).broadcast_to([P, B_HEADS, B_HV])
                after(did(dve.tensor_tensor(o3, bank_pair(2 * h).rearrange("p (g v) -> p g v", g=B_HEADS), inv, ALU.mult)))
                after(did(dve.tensor_tensor(o3, o3, bnorm_row[:, :].unsqueeze(1).broadcast_to([P, B_HEADS, B_HV]), ALU.mult)))
                dve.wait_ge(silu_done, h + 1)
                dve.tensor_tensor(bo[:, h, :], bo[:, h, :], br[:, h, :], ALU.mult).then_inc(o_ready, 1)
            for h in range(TT):
                dve.wait_ge(oT_hi_ready, h + 1)
                cols = slice(h * P, (h + 1) * P)
                dve.tensor_tensor(hT_lo[:, :, cols], bank_pair(4 + 2 * h).rearrange("p (a b) -> p a b", a=KB),
                                  hT_hi[:, :, cols].bitcast(F32), ALU.subtract).then_inc(oT_lo_ready, 1)
            for n in range(BOUT + 2, WQ[1] + 2):
                lo_at(n)
            add_to_x(3, 0, WQ[1] - 1)
            peer(1)
            add_to_x(4, 4, TILES - 1)
            norm(4)

        @block.tensor
        def _(pe):
            def product(o, a, b, start=False, stop=False):
                return pe.matmul(o, a, b, start=start, stop=stop, skip_group_check=True)

            def stationary_tile(slot, ready, bank, rest_ready):
                w_h, w_l = tile_hi[slot], tile_lo[slot]
                o = psum[:, bank, 0:T]
                pe.wait_ge(hi_ready, ready)
                for kb in range(KB):
                    w = w_h[:, kb * P:(kb + 1) * P]
                    product(o, w, hT_hi[:, kb, :], start=kb == 0)
                    product(o, w, hT_lo[:, kb, :])
                pe.wait_ge(*rest_ready)
                for kb in range(KB):
                    ins = product(o, w_l[:, kb * P:(kb + 1) * P], hT_hi[:, kb, :], stop=kb == KB - 1)
                ins.then_inc(tile_used, 1)

            def moving_tile(slot, ready, rest_ready, first_bank, a_hi, a_lo, start, stop, a_lo_ready=None):
                pe.wait_ge(hi_ready, ready)
                for a, first in ((a_hi, start), (a_lo, False)):
                    if a is a_lo and a_lo_ready is not None:
                        pe.wait_ge(*a_lo_ready)
                    for h in range(TT):
                        cols = slice(h * P, (h + 1) * P)
                        for d in range(2):
                            product(psum[:, first_bank + 2 * h + d, :], a[:, cols], tile_hi[slot][:, d * BANK:(d + 1) * BANK], start=first)
                pe.wait_ge(lo_ready, rest_ready)
                for h in range(TT):
                    cols = slice(h * P, (h + 1) * P)
                    for d in range(2):
                        ins = product(psum[:, first_bank + 2 * h + d, :], a_hi[:, cols], tile_lo[slot][:, d * BANK:(d + 1) * BANK], stop=stop)
                ins.then_inc(tile_used, 1)

            def turn(src, first_bank, blocks):
                for b in range(blocks):
                    ins = pe.transpose(psum[:, first_bank + b // 4, (b % 4) * P:(b % 4 + 1) * P], src[:, b * P:(b + 1) * P], ident)
                return ins

            def norm(i):
                for h in range(TT):
                    pe.wait_ge(hn_ready[i], h + 1)
                    turn(hn[:, h, :], 2 * h, KB).then_inc(hn_turned[i], 1)

            pe.wait_ge(consts_loaded, 16 * 2)
            norm(0)
            pe.wait_ge(hT_lo_ready[0], TT)
            for j in range(A_BLOCKS):
                if j >= 2:
                    pe.wait_ge(ain_biased, 4 * (j - 1))
                for kb in range(KB):
                    n = AIN + j * KB + kb
                    moving_tile(n % 2, n + 1, lo_count(n), 4 * (j % 2), hT_hi[:, kb, :], hT_lo[:, kb, :], kb == 0, kb == KB - 1)
            pe.wait_ge(v_normed, TT)
            pe.wait_ge(ws_masked, 1)
            for h in range(TT):
                pe.wait_ge(ain_biased, 4 * (3 + h))
                for g in range(A_GROUPS):
                    ins = product(psum[:, 4 * h + g // 2, (g % 2) * A_GDIM:(g % 2 + 1) * A_GDIM], wsT[:, g, :],
                                  zv[:, h, g * A_GDIM:(g + 1) * A_GDIM], start=True, stop=True)
                ins.then_inc(sv_done, 1)
            for h in range(TT):
                pe.wait_ge(y_ready, A_GROUPS * (h + 1))
                turn(zu[:, h, :], 4 * h, YB).then_inc(y_turned, 1)
            pe.wait_ge(yT_lo_ready, 4 * TT)
            for kb in range(YB):
                n = AOUT + kb
                moving_tile(n % 2, n + 1, lo_count(n), 0, yT_hi[:, kb, :], yT_lo[:, kb, :], kb == 0, kb == YB - 1)

            def peer(l):
                norm(1 + 2 * l)
                pe.wait_ge(hT_lo_ready[1 + 2 * l], TT)
                for c in range(RAW_SLOTS):
                    n = WQ[l] + c
                    stationary_tile(n % 2, n + 1, c, (lo_ready, lo_count(n)))
                with pe.Fori(1, N_WQ // RAW_SLOTS) as i:
                    for c in range(RAW_SLOTS):
                        pe.wait_ge(q_copied[l], i * RAW_SLOTS + (c + 1 - RAW_SLOTS))
                        stationary_tile(c % 2, i * RAW_SLOTS + (WQ[l] + c + 1), c,
                                        (lo_ready, i * RAW_SLOTS + lo_count(WQ[l] + c)))
                pe.wait_ge(q_copied[l], N_WQ)
                pe.wait_ge(small_loaded, 16 * N_SMALL)
                for h in range(TT):
                    for r in range(P_ROWS):
                        ins = product(psum[:, 4 * h + r // 4, (r % 4) * NK:(r % 4 + 1) * NK], qT[:, r, h * P:(h + 1) * P],
                                      keysT[:, l, r % 2, :], start=True, stop=True)
                        if r % 4 == 3:
                            ins.then_inc(scores_done[l], 1)
                for c in range(RAW_SLOTS):
                    pe.wait_ge(scores_copied[l], c + 1)
                    stationary_tile(c % 2, UT[l] + c + 1, c, (lo_ready, lo_count(UT[l] + c)))

                def expert_tile(i, c, rest=None):
                    pe.wait_ge(gelu_done[l], i * RAW_SLOTS + (c + 1 - RAW_SLOTS))
                    stationary_tile(c % 2, i * RAW_SLOTS + (UT[l] + c + 1), c,
                                    rest or (lo_ready, i * RAW_SLOTS + lo_count(UT[l] + c)))

                with pe.Fori(1, TURN_AT // RAW_SLOTS) as i:
                    for c in range(RAW_SLOTS):
                        expert_tile(i, c)
                pe.wait_ge(scores_copied[l], 4 * TT)
                pe.wait_ge(gates_ready[l], TT)
                for k in range(3):
                    for h in range(TT):
                        c = 2 * k + h
                        ins = pe.transpose(psum[:, 4 + c // 4, (c % 4) * P:(c % 4 + 1) * P], picks[:, h, k, :], ident)
                ins.then_inc(picks_turned[l], 1)
                with pe.Fori(TURN_AT // RAW_SLOTS, (N_EXP - N_LATE) // RAW_SLOTS) as i:
                    for c in range(RAW_SLOTS):
                        expert_tile(i, c)

                def gate_matrices(g, ready, bank_out):
                    pe.wait_ge(onehot1_ready[l], ready)
                    pe.wait_ge(onehot2_ready[l], ready)
                    if bank_out is not None:
                        pe.wait_ge(gated[l], bank_out)
                    for c in range(GROUP):
                        ins = product(psum[:, 4 + g % 4, c * P:(c + 1) * P], onehot1[:, g % 2, c, :], onehot2[:, g % 2, c, :],
                                      start=True, stop=True)
                    ins.then_inc(gmat_done[l], 1)

                pe.wait_ge(picksT_ready[l], 2)
                for c in range(RAW_SLOTS):
                    for g in (2 * c, 2 * c + 1):
                        gate_matrices(g, g + 1, g - 3 if g >= 4 else None)
                    expert_tile((N_EXP - N_LATE) // RAW_SLOTS, c, (late_lo_ready[l], c + 1))
                with pe.Fori(1, N_LATE // RAW_SLOTS) as i:
                    for c in range(RAW_SLOTS):
                        for g in (2 * c, 2 * c + 1):
                            gate_matrices(g, i * 8 + (g + 1), i * 8 + (g - 3))
                        expert_tile(i + (N_EXP - N_LATE) // RAW_SLOTS, c, (late_lo_ready[l], i * RAW_SLOTS + (c + 1)))

                def value_tile(slot, ready, rest_ready, k, start, stop):
                    pe.wait_ge(w_hi_ready[l], k + 1)
                    moving_tile(slot, ready, rest_ready, 4, w_hi[slot], w_lo[slot], start, stop, (w_lo_ready[l], k + 1))

                for k in range(RAW_SLOTS):
                    value_tile(k % 2, VT[l] + k + 1, lo_count(VT[l] + k), k, k == 0, False)
                with pe.Fori(1, N_EXP // RAW_SLOTS - 1) as i:
                    for c in range(RAW_SLOTS):
                        value_tile(c % 2, i * RAW_SLOTS + (VT[l] + c + 1), i * RAW_SLOTS + lo_count(VT[l] + c), i * RAW_SLOTS + c, False, False)
                for k in range(N_EXP - RAW_SLOTS, N_EXP):
                    value_tile(k % 2, VT[l] + k + 1, lo_count(VT[l] + k), k, False, k == N_EXP - 1)

            peer(0)
            norm(2)
            pe.wait_ge(hT_lo_ready[2], TT)
            pe.wait_ge(gla_loaded, 16 * 5)
            for kb in range(KB):
                ins = product(psum[0:B_RANK, 4, 0:T], w_g[:, kb, :], hT[:, kb, :], start=kb == 0, stop=kb == KB - 1)
            ins.then_inc(glr_done, 1)
            for c in range(N_BQK):
                n = BQK + c
                if c >= 4:
                    pe.wait_ge(qk_copied, c - 3)
                stationary_tile(n % 2, n + 1, c % 4, (lo_ready, lo_count(n)))
                if c == 0:
                    pe.wait_ge(glr_copied, 1)
                    for h in range(TT):
                        product(psum[:, 5 + h, :], g_lrT[:, h * P:(h + 1) * P], w_g2[:, :], start=True, stop=True).then_inc(la_done, 1)
                if c == 5:
                    pe.wait_ge(la_ready, 1)
                    for d in range(B_HEADS):
                        for h in range(TT):
                            ins = product(psum[:, 5 + d // 2, (d % 2) * T + h * P:(d % 2) * T + (h + 1) * P],
                                          z_la[:, h, d * B_HK:(d + 1) * B_HK], tri16, start=True, stop=True)
                    ins.then_inc(gcum_done, 1)

            def level(L):
                q, k = (gq, gk) if L == 0 else (qe[L % 2], ke[L % 2])
                if L == 0:
                    pe.wait_ge(qk_copied, 2 * B_HEADS)
                else:
                    pe.wait_ge(qk_decayed, L)
                if L == 1:
                    pe.wait_ge(gcum_copied, 1)
                if L >= 2:
                    pe.wait_ge(level_kept, L - 1)
                first = 4 + 2 * (L % 2)
                for d in range(B_HEADS):
                    if L == 1:
                        ins = product(psum[:, first, d * P:(d + 1) * P], k[:, d, 0:P], q[:, d, P:T], start=True, stop=True)
                        continue
                    for h in range(TT):
                        c = TT * d + h
                        ins = product(psum[:, first + c // 4, (c % 4) * P:(c % 4 + 1) * P], k[:, d, h * P:(h + 1) * P],
                                      q[:, d, h * P:(h + 1) * P], start=True, stop=True)
                ins.then_inc(level_done, 1)

            for c in range(N_BVR):
                n = BVR + c
                if c == 0:
                    pe.wait_ge(qk_copied, 2 * B_HEADS)
                    pe.wait_ge(gcum_copied, 1)
                    level(0)
                if c == KB:
                    pe.wait_ge(bv_copied, 4)
                kb = c % KB
                moving_tile(n % 2, n + 1, lo_count(n), 0, hT_hi[:, kb, :], hT_lo[:, kb, :], kb == 0, kb == KB - 1)
                if c % 2 == 1:
                    level(c // 2 + 1)
            pe.wait_ge(level_kept, B_LEVELS + 2)
            pe.wait_ge(silu_done, TT)
            for h in range(TT):
                for d in range(B_HEADS):
                    o = psum[:, 2 * h + d // 2, (d % 2) * B_HV:(d % 2 + 1) * B_HV]
                    if h == 1:
                        product(o, score_x[:, d, :], bv[:, 0, d * B_HV:(d + 1) * B_HV], start=True)
                    ins = product(o, score_in[:, TT * d + h, :], bv[:, h, d * B_HV:(d + 1) * B_HV], start=h == 0, stop=True)
                ins.then_inc(o_done, 1)
            for h in range(TT):
                pe.wait_ge(o_ready, h + 1)
                turn(bo[:, h, :], 4 + 2 * h, KB).then_inc(o_turned, 1)
            pe.wait_ge(oT_lo_ready, TT)
            for kb in range(KB):
                n = BOUT + kb
                moving_tile(n % 2, n + 1, lo_count(n), 0, hT_hi[:, kb, :], hT_lo[:, kb, :], kb == 0, kb == KB - 1)
            peer(1)


def _layout(i):
    a = {k: np.asarray(v) for k, v in i.items()}

    def moving(w, blocks):
        kb = w.shape[0] // P
        return w.reshape(kb, P, blocks, TILE).transpose(2, 0, 1, 3).reshape(blocks * kb, P, TILE)

    def stationary(w):
        n = w.shape[1] // P
        return w.reshape(KB, P, n, P).transpose(2, 1, 0, 3).reshape(n, P, TILE)

    s, tk = np.arange(P)[:, None], np.arange(P)[None, :]
    masks = [((s ^ tk) >> j == 1) & (tk > s) for j in range(B_LEVELS)] + [s == tk]
    b_w = a["b_w_in"][0]
    v_first = np.concatenate([a["a_w_in"][0][:, A_WIDTH:], a["a_w_in"][0][:, :A_WIDTH]], axis=1)
    r = {
        "x": a["x"][0],
        "a_in": moving(v_first, A_BLOCKS),
        "a_out": moving(a["a_w_out"][0], 1),
        "b_in": np.concatenate([a["a_b_in"][0][A_WIDTH:], a["a_b_in"][0][:A_WIDTH]]),
        "ln_g": a["a_ln_g"][0],
        "ln_b": a["a_ln_b"][0],
        "w_sT": a["a_w_s"][0].transpose(2, 0, 1),
        "b_sT": a["a_b_s"][0].T,
        "gains": np.stack([a[k][l].reshape(KB, P).T for l in range(2) for k in ("norm_mix", "norm_ffn")], axis=1),
        "final_norm": a["final_norm"],
        "keysT": np.stack([np.stack([a[k][l].T for k in ("p_k1", "p_k2")], axis=1) for l in range(2)], axis=1),
        "b_qk": stationary(b_w[:, :2 * B_KEY]),
        "b_vr": moving(b_w[:, 2 * B_KEY:2 * B_KEY + 2 * D], 2),
        "w_g": b_w[:, 2 * B_KEY + 2 * D:].reshape(KB, P, B_RANK).transpose(1, 0, 2),
        "w_g2": a["b_w_g2"][0],
        "b_g": a["b_b_g"][0],
        "b_norm": a["b_norm"][0],
        "b_out": moving(a["b_w_out"][0], 1),
        "consts": np.stack([np.eye(P), np.broadcast_to(np.arange(P), (P, P)), (s <= tk) / 16.0], axis=1).astype(np.float32),
        "masks": np.stack(masks, axis=1).astype(np.uint32),
    }
    for l in range(2):
        r[f"w_q{l}"] = stationary(a["p_w_q"][l])
        r[f"u{l}"] = a["p_u"][l].reshape(NK, NK, KB, P).transpose(1, 3, 2, 0).reshape(NK, P, TILE)
        r[f"v{l}"] = a["p_v"][l].reshape(NK, NK, D).transpose(1, 0, 2)
    return {k: np.ascontiguousarray(v) for k, v in r.items()}


def kernel(**inputs):
    import concourse.bacc as bacc
    from concourse.bass_utils import run_bass_kernel_spmd

    arrays = _layout(inputs)
    nc = bacc.Bacc("TRN2", target_bir_lowering=False, num_devices=1)
    t = {k: nc.dram_tensor(f"in_{k}", v.shape, mybir.dt.from_np(v.dtype), kind="ExternalInput").ap() for k, v in arrays.items()}
    out = nc.dram_tensor("out_0", (TT, P, D), F32, kind="ExternalOutput").ap()
    trunk(nc, t, out)
    r = run_bass_kernel_spmd(nc, [{f"in_{k}": v for k, v in arrays.items()}], core_ids=[0])
    return r.results[0]["out_0"].reshape(1, T, D)
```

```python
from contextlib import ExitStack

import numpy as np

import concourse.bass as bass
from concourse import mybir

F32 = mybir.dt.float32
F32R = mybir.dt.float32r
BF16 = mybir.dt.bfloat16
U32 = mybir.dt.uint32
ALU = mybir.AluOpType
ACT = mybir.ActivationFunctionType
AX = mybir.AxisListType

P = 128
D = 1024
KB = D // P
T = 256
TT = T // P
TILE = 1024
BANK = 512
EPS = 1e-6

A_WIDTH = 2048
A_GROUPS = 8
A_GDIM = A_WIDTH // A_GROUPS
A_BLOCKS = 2 * A_WIDTH // TILE
YB = A_WIDTH // P

B_HEADS = 4
B_HK = 128
B_HV = 256
B_KEY = B_HEADS * B_HK
B_RANK = 16
B_LEVELS = 7

P_HEADS = 8
P_ROWS = 2 * P_HEADS
NK = 128
TOPK = 16
PICKS = P_HEADS * TOPK
N_SMALL = 5

GROUP = 4
GROUPS = T // GROUP
EXP_AT = 84
TURN_AT = 88
N_LATE = GROUPS // 2

RAW_SLOTS = 4
SPLIT_SLOTS = 2
LOWEST = -3.0e38

N_AIN = A_BLOCKS * KB
N_AOUT = YB
N_WQ = P_ROWS
N_EXP = NK
N_BQK = 2 * B_KEY // P
N_BRV = 2 * KB
N_BOUT = KB
AIN = 0
AOUT = AIN + N_AIN
WQ = [AOUT + N_AOUT, 0]
UT = [WQ[0] + N_WQ, 0]
VT = [UT[0] + N_EXP, 0]
BQK = VT[0] + N_EXP
BRV = BQK + N_BQK
BOUT = BRV + N_BRV
WQ[1] = BOUT + N_BOUT
UT[1] = WQ[1] + N_WQ
VT[1] = UT[1] + N_EXP
TILES = VT[1] + N_EXP


def lo_count(n):
    return n + 1 - N_LATE * sum(n >= VT[l] for l in range(2))


def trunk(nc, t, out):
    with ExitStack() as ctx:
        def sb(name, shape, dt=F32):
            return ctx.enter_context(nc.sbuf_tensor(name, shape, dt))

        def sem(name):
            return ctx.enter_context(nc.semaphore(name))

        raw = [sb(f"raw{s}", [P, TILE]) for s in range(RAW_SLOTS)]
        tile_hi = [sb(f"tile_hi{s}", [P, TILE], F32R) for s in range(SPLIT_SLOTS)]
        tile_lo = [sb(f"tile_lo{s}", [P, TILE], F32R) for s in range(SPLIT_SLOTS)]
        hT_hi = sb("hT_hi", [P, KB, T], F32R)
        hT_lo = sb("hT_lo", [P, KB, T], F32R)
        x = sb("x", [P, TT, D])
        consts = sb("consts", [P, 3, P])
        ident, iota, tri16 = consts[:, 0, :], consts[:, 1, :], consts[:, 2, :]
        keysT = sb("keysT", [P, 2, 2, NK])
        b_sT = sb("b_sT", [P, A_GROUPS])
        picks = sb("picks", [P, TT, 3, PICKS])
        picksT = sb("picksT", [P, 3, T])
        sumsq = sb("sumsq", [P, TT])
        meansq = sb("meansq", [P, TT])
        rms = sb("rms", [P, TT])
        rstd = sb("rstd", [P, TT])
        v_sum = sb("v_sum", [P, TT, 2])
        v_mean = sb("v_mean", [P, TT])
        head_sum = sb("head_sum", [P, TT, P_HEADS])
        head_inv = sb("head_inv", [P, TT, P_HEADS])

        def overlay(parts):
            with ExitStack() as own:
                return [own.enter_context(nc.sbuf_tensor(*p)) for p in parts]

        onehot1, onehot2 = overlay([("onehot1", [P, 2, GROUP, P], F32), ("onehot2", [P, 2, GROUP, P], F32)])
        (topv, topi, topi_f, candv, candpos, pos_a, pos_b, pos_af, pos_bf) = overlay([
            ("topv", [P, TT, P_ROWS, TOPK], F32),
            ("topi", [P, TT, P_ROWS, TOPK], U32),
            ("topi_f", [P, P_ROWS, TOPK], F32),
            ("candv", [P, P_HEADS, TOPK], F32),
            ("candpos", [P, P_HEADS, TOPK], U32),
            ("pos_a", [P, P_HEADS, TOPK], U32),
            ("pos_b", [P, P_HEADS, TOPK], U32),
            ("pos_af", [P, P_HEADS, TOPK], F32),
            ("pos_bf", [P, P_HEADS, TOPK], F32),
        ])
        (gain_row,) = overlay([("gain_row", [P, D], F32)])
        sb("reserved_small", [P, 2048])
        equal2, gelu_out = overlay([("equal2", [P, 2, P, GROUP], BF16), ("gelu_out", [P, 2, T], F32)])
        w_hi0, w_hi1, w_lo0, w_lo1 = overlay([(f"w_{n}", [P, T], F32R) for n in ("hi0", "hi1", "lo0", "lo1")])
        w_hi, w_lo = [w_hi0, w_hi1], [w_lo0, w_lo1]
        sb("reserved_w", [P, 4 * T])
        numbers16 = sb("numbers16", [P, P, GROUP], BF16)
        picks16 = sb("picks16", [P, T], BF16)

        (acts,) = overlay([("acts", [P, NK, T], F32)])
        (_, scores, qT) = overlay([
            ("pad_scores", [P, 96 * T], F32),
            ("scores", [P, TT, P_ROWS, NK], F32),
            ("qT", [P, P_ROWS, T], F32),
        ])
        (_, cand, look) = overlay([
            ("pad_cand", [P, 112 * T], F32),
            ("cand", [P, P_HEADS, TOPK * TOPK], F32),
            ("look", [P, P_HEADS, TOPK, TOPK], F32),
        ])
        (b_in, ln_g, ln_b, zv, zu, wsT, yT_hi, yT_lo) = overlay([
            ("b_in", [P, 2 * A_WIDTH], F32),
            ("ln_g", [P, A_WIDTH], F32),
            ("ln_b", [P, A_WIDTH], F32),
            ("zv", [P, TT, A_WIDTH], F32),
            ("zu", [P, TT, A_WIDTH], F32),
            ("wsT", [P, A_GROUPS, P], F32),
            ("yT_hi", [P, YB, T], F32R),
            ("yT_lo", [P, YB, T], F32R),
        ])
        (gq, gk, gcum, z_la, z_tmp, ed0, ed1, qe0, qe1, ke0, ke1, score_in, score_x, bv, br, bsg, bo, bg_row,
         bnorm_row, w_g2, w_g, w_g_hi, w_g_lo, masks, g_lrT, head_ms) = overlay([
            ("gq", [P, B_HEADS, T], F32),
            ("gk", [P, B_HEADS, T], F32),
            ("gcum", [P, B_HEADS, T], F32),
            ("z_la", [P, TT, B_KEY], F32),
            ("z_tmp", [P, TT, B_KEY], F32),
            ("ed0", [P, B_HEADS, T], F32),
            ("ed1", [P, B_HEADS, T], F32),
            ("qe0", [P, B_HEADS, T], F32),
            ("qe1", [P, B_HEADS, T], F32),
            ("ke0", [P, B_HEADS, T], F32),
            ("ke1", [P, B_HEADS, T], F32),
            ("score_in", [P, B_HEADS * TT, P], F32),
            ("score_x", [P, B_HEADS, P], F32),
            ("bv", [P, TT, D], F32),
            ("br", [P, TT, D], F32),
            ("bsg", [P, TT, D], F32),
            ("bo", [P, TT, D], F32),
            ("bg_row", [P, B_KEY], F32),
            ("bnorm_row", [P, B_HV], F32),
            ("w_g2", [B_RANK, B_KEY], F32),
            ("w_g", [P, KB, B_RANK], F32),
            ("w_g_hi", [P, KB, B_RANK], F32R),
            ("w_g_lo", [P, KB, B_RANK], F32R),
            ("masks", [P, B_LEVELS + 1, P], U32),
            ("g_lrT", [B_RANK, T], F32),
            ("head_ms", [P, TT, 4, B_HEADS], F32),
        ])
        ed, qe, ke = [ed0, ed1], [qe0, qe1], [ke0, ke1]
        (_, hn) = overlay([("pad_norm", [P, 112 * T], F32), ("hn", [P, TT, D], F32)])

        psum = ctx.enter_context(nc.psum_tensor("psum", [P, 8, BANK], F32))

        raw_loaded = [sem(f"raw_loaded{s}") for s in range(RAW_SLOTS)]
        hi_ready, lo_ready, tile_used = sem("hi_ready"), sem("lo_ready"), sem("tile_used")
        numbers_ready = sem("numbers_ready")
        consts_loaded = sem("consts_loaded")
        x_loaded = [sem(f"x_loaded{h}") for h in range(TT)]
        gain_loaded = [sem(f"gain_loaded{i}") for i in range(5)]
        b_in_loaded = [sem(f"b_in_loaded{k}") for k in range(2)]
        v_scaled = sem("v_scaled")
        small_loaded, w_g_loaded, gla_loaded = sem("small_loaded"), sem("w_g_loaded"), sem("gla_loaded")
        w_g_hi_ready, w_g_lo_ready = sem("w_g_hi_ready"), sem("w_g_lo_ready")
        half_done = [sem(f"half_done{i}") for i in range(5)]
        ws_masked = sem("ws_masked")
        dve_chain = sem("dve_chain")
        x_ready = [sem(f"x_ready{i}") for i in range(5)]
        squares = [sem(f"squares{i}") for i in range(5)]
        ms_ready = [sem(f"ms_ready{i}") for i in range(5)]
        rms_ready = [sem(f"rms_ready{i}") for i in range(5)]
        hn_ready = [sem(f"hn_ready{i}") for i in range(5)]
        hn_turned = [sem(f"hn_turned{i}") for i in range(4)]
        hT_hi_ready = [sem(f"hT_hi_ready{i}") for i in range(4)]
        hT_lo_ready = [sem(f"hT_lo_ready{i}") for i in range(4)]
        ain_biased, ain_gelu = sem("ain_biased"), sem("ain_gelu")
        v_centred, v_squares, v_ms, v_std, v_normed = sem("v_centred"), sem("v_squares"), sem("v_ms"), sem("v_std"), sem("v_normed")
        sv_done, y_ready, y_turned, yT_hi_ready, yT_lo_ready = sem("sv_done"), sem("y_ready"), sem("y_turned"), sem("yT_hi_ready"), sem("yT_lo_ready")
        q_copied = [sem(f"q_copied{l}") for l in range(2)]
        scores_done = [sem(f"scores_done{l}") for l in range(2)]
        scores_copied = [sem(f"scores_copied{l}") for l in range(2)]
        gelu_done = [sem(f"gelu_done{l}") for l in range(2)]
        shifted = [sem(f"shifted{l}") for l in range(2)]
        exps = [sem(f"exps{l}") for l in range(2)]
        gates_ready = [sem(f"gates_ready{l}") for l in range(2)]
        picks_turned = [sem(f"picks_turned{l}") for l in range(2)]
        picksT_ready = [sem(f"picksT_ready{l}") for l in range(2)]
        ones_ready = [sem(f"ones_ready{l}") for l in range(2)]
        equal2_ready = [sem(f"equal2_ready{l}") for l in range(2)]
        onehot1_ready = [sem(f"onehot1_ready{l}") for l in range(2)]
        onehot2_ready = [sem(f"onehot2_ready{l}") for l in range(2)]
        late_lo_ready = [sem(f"late_lo_ready{l}") for l in range(2)]
        late_gated = [sem(f"late_gated{l}") for l in range(2)]
        gmat_done = [sem(f"gmat_done{l}") for l in range(2)]
        gated = [sem(f"gated{l}") for l in range(2)]
        w_hi_ready = [sem(f"w_hi_ready{l}") for l in range(2)]
        w_lo_ready = [sem(f"w_lo_ready{l}") for l in range(2)]
        glr_done, glr_copied, la_done, z_ready, la_abs, la_exp, la_ln, la_ready = (
            sem("glr_done"), sem("glr_copied"), sem("la_done"), sem("z_ready"), sem("la_abs"), sem("la_exp"), sem("la_ln"), sem("la_ready"))
        gcum_done, gcum_copied, qk_copied = sem("gcum_done"), sem("gcum_copied"), sem("qk_copied")
        score_zeroed, diff_ready, decay_ready, qk_decayed, level_done, level_kept = (
            sem("score_zeroed"), sem("diff_ready"), sem("decay_ready"), sem("qk_decayed"), sem("level_done"), sem("level_kept"))
        br_copied, br_normed = sem("br_copied"), sem("br_normed")
        bv_copied, sig_done, silu_done, o_done, o_squares, o_ms, o_rms, o_ready, o_turned, oT_hi_ready, oT_lo_ready = (
            sem("bv_copied"), sem("sig_done"), sem("silu_done"), sem("o_done"), sem("o_squares"), sem("o_ms"), sem("o_rms"),
            sem("o_ready"), sem("o_turned"), sem("oT_hi_ready"), sem("oT_lo_ready"))
        stored = sem("stored")

        def bank_pair(b, n=2):
            return psum[:, b:b + n, :].rearrange("p b c -> p (b c)")

        block = ctx.enter_context(nc.Block())

        @block.sync
        def _(sp):
            for h in range(TT):
                sp.dma_start(x[:, h, :], t["x"][h * P:(h + 1) * P]).then_inc(x_loaded[h], 16)
            sp.dma_start(consts[:, :, :], t["consts"]).then_inc(consts_loaded, 16)

            def load(src, slot):
                sp.dma_start(raw[slot][:, :], src).then_inc(raw_loaded[slot], 16)

            def stage(name, first, start, end, made=lo_ready, offset=None):
                if offset is None:
                    offset = lo_count(first + start - RAW_SLOTS) - (start - RAW_SLOTS)
                with sp.Fori(start // RAW_SLOTS, end // RAW_SLOTS) as i:
                    for s in range(RAW_SLOTS):
                        sp.wait_ge(made, i * RAW_SLOTS + (offset + s - RAW_SLOTS))
                        load(t[name][i * RAW_SLOTS + s], s)

            for s in range(RAW_SLOTS):
                load(t["a_in"][s], s)
            stage("a_in", AIN, RAW_SLOTS, N_AIN)
            stage("a_out", AOUT, 0, N_AOUT)
            for l in range(2):
                stage(f"w_q{l}", WQ[l], 0, N_WQ)
                early = N_EXP - N_LATE
                stage(f"u{l}", UT[l], 0, early + RAW_SLOTS)
                stage(f"u{l}", UT[l], early + RAW_SLOTS, N_EXP, late_lo_ready[l], 1 - early)
                for s in range(RAW_SLOTS):
                    sp.wait_ge(late_lo_ready[l], N_LATE - RAW_SLOTS + s + 1)
                    load(t[f"v{l}"][s], s)
                stage(f"v{l}", VT[l], RAW_SLOTS, N_EXP)
                if l == 0:
                    stage("b_qk", BQK, 0, N_BQK)
                    stage("b_rv", BRV, 0, N_BRV)
                    stage("b_out", BOUT, 0, N_BOUT)
            for b in range(2 * TT):
                h, cols = b // 2, slice(b % 2 * BANK, b % 2 * BANK + BANK)
                sp.wait_ge(hn_ready[4], b + 1)
                sp.dma_start(out[h][:, cols], hn[:, h, cols]).then_inc(stored, 16)
            sp.wait_ge(stored, 16 * 2 * TT)

        @block.gpsimd
        def _(pool):
            def load_gain(i, free, count):
                if free is not None:
                    pool.wait_ge(free, count)
                pool.dma_start(gain_row[:, :], t["gains"][i].partition_broadcast(P)).then_inc(gain_loaded[i], 16)

            load_gain(0, None, 0)
            pool.wait_ge(hn_ready[0], 1)
            pool.dma_start(b_in[:, 0:A_WIDTH], t["b_in"][0:A_WIDTH].partition_broadcast(P)).then_inc(b_in_loaded[0], 16)
            pool.wait_ge(hi_ready, 10)
            pool.dma_start(ln_g[:, :], t["ln_g"].partition_broadcast(P)).then_inc(small_loaded, 16)
            pool.wait_ge(hi_ready, 13)
            pool.dma_start(b_in[:, A_WIDTH:], t["b_in"][A_WIDTH:].partition_broadcast(P)).then_inc(b_in_loaded[1], 16)
            pool.wait_ge(hi_ready, 16)
            pool.dma_start(ln_b[:, :], t["ln_b"].partition_broadcast(P)).then_inc(small_loaded, 16)
            pool.wait_ge(hi_ready, 19)
            for dst, src in ((wsT[:, :, :], t["w_sT"]), (b_sT[:, :], t["b_sT"]), (keysT[:, :, :, :], t["keysT"])):
                pool.dma_start(dst, src).then_inc(small_loaded, 16)
            pool.wait_ge(small_loaded, 16 * N_SMALL)
            pool.affine_select(out=wsT[:, :, :], in_=wsT[:, :, :], compare_op=ALU.is_ge, fill=0.0, base=0,
                               pattern=[[0, A_GROUPS], [1, P]], channel_multiplier=-1).then_inc(ws_masked, 1)

            def late_experts(l):
                pool.wait_ge(shifted[l], TT)
                pool.memset(acts[:, N_EXP - N_LATE:N_EXP, :], 1.0).then_inc(ones_ready[l], 1)
                first = UT[l] + N_EXP - N_LATE
                with pool.Fori(0, N_LATE // RAW_SLOTS) as i:
                    for c in range(RAW_SLOTS):
                        pool.wait_ge(hi_ready, i * RAW_SLOTS + (first + c + 1))
                        pool.tensor_tensor(tile_lo[c % SPLIT_SLOTS][:, :], raw[c][:, :], tile_hi[c % SPLIT_SLOTS][:, :].bitcast(F32),
                                           ALU.subtract).then_inc(late_lo_ready[l], 1)

            for c in range(2 * TT):
                h, cols = c // 2, slice(c % 2 * TILE, c % 2 * TILE + TILE)
                pool.wait_ge(v_scaled, c + 1)
                pool.tensor_tensor(zv[:, h, cols], zv[:, h, cols], ln_b[:, cols], ALU.add).then_inc(v_normed, 1)
            load_gain(1, hn_ready[0], 2 * TT)
            late_experts(0)
            load_gain(2, gmat_done[0], GROUPS)
            pool.wait_ge(x_ready[2], 4)
            pool.dma_start(w_g[:, :, :], t["w_g"]).then_inc(w_g_loaded, 16)
            gla = [(masks[:, :, :], t["masks"]), (w_g2[:, :], t["w_g2"]),
                   (bg_row[:, :], t["b_g"].partition_broadcast(P)), (bnorm_row[:, :], t["b_norm"].partition_broadcast(P))]
            for dst, src in gla:
                pool.dma_start(dst, src).then_inc(gla_loaded, 16)
            pool.memset(score_in[:, :, :], 0.0).then_inc(score_zeroed, 1)

            def diff(L):
                if L >= 3:
                    pool.wait_ge(qk_decayed, L - 2)
                e = ed[L % 2]
                if L == 1:
                    last = gcum[:, :, P - 1:P].broadcast_to([P, B_HEADS, P])
                    pool.tensor_tensor(e[:, :, 0:P], last, gcum[:, :, 0:P], ALU.subtract).then_inc(diff_ready, 1)
                    return
                m = 1 << (L - 2)
                g4 = gcum[:, :, :].rearrange("p h (b w m) -> p (h b) w m", w=2, m=m)
                e4 = e[:, :, :].rearrange("p h (b w m) -> p (h b) w m", w=2, m=m)
                ref = g4[:, :, 0, m - 1:m].broadcast_to([P, B_HEADS * T // (2 * m), m])
                pool.tensor_tensor(e4[:, :, 0, :], ref, g4[:, :, 0, :], ALU.subtract)
                pool.tensor_tensor(e4[:, :, 1, :], g4[:, :, 1, :], ref, ALU.subtract).then_inc(diff_ready, 1)

            pool.wait_ge(gcum_copied, 1)
            for L in range(1, B_LEVELS + 2):
                diff(L)
            pool.wait_ge(br_copied, 4)
            for h in range(TT):
                g3 = br[:, h, :].rearrange("p (g v) -> p g v", g=B_HEADS)
                o3 = bo[:, h, :].rearrange("p (g v) -> p g v", g=B_HEADS)
                pool.tensor_tensor(o3, g3, bnorm_row[:, :].unsqueeze(1).broadcast_to([P, B_HEADS, B_HV]), ALU.mult).then_inc(br_normed, 1)
            load_gain(3, hn_ready[2], 2 * TT)
            late_experts(1)
            load_gain(4, gmat_done[1], GROUPS)

        @block.scalar
        def _(act):
            def hi(slot, raw_count, used):
                act.wait_ge(raw_loaded[slot], raw_count)
                if used is not None:
                    act.wait_ge(tile_used, used)
                act.activation(tile_hi[slot % SPLIT_SLOTS][:, :], raw[slot][:, :], ACT.Copy).then_inc(hi_ready, 1)

            def hi_at(n):
                hi(n % RAW_SLOTS, 16 * (n // RAW_SLOTS + 1), n - 1 if n >= SPLIT_SLOTS else None)

            def hi_in(i, c, first):
                n = first + c
                hi(n % RAW_SLOTS, i * 16 + 16 * (n // RAW_SLOTS + 1), i * RAW_SLOTS + (n - 1))

            def norm(i, after_sums):
                act.preload_act_table(ACT.Sqrt)
                for h in range(TT):
                    if i == 0:
                        act.wait_ge(x_loaded[h], 16)
                    else:
                        act.wait_ge(x_ready[i], 2 * h + 2)
                    act.activation(hn[:, h, :], x[:, h, :], ACT.Square, accum_out=sumsq[:, h:h + 1]).then_inc(squares[i], 1)
                    act.wait_ge(ms_ready[i], h + 1)
                    act.activation(rms[:, h:h + 1], meansq[:, h:h + 1], ACT.Sqrt).then_inc(rms_ready[i], 1)
                if i == 4:
                    return
                for n in after_sums:
                    hi_at(n)
                for b in range(2 * TT):
                    h, half = b // 2, b % 2
                    act.wait_ge(hn_turned[i], b + 1)
                    act.activation(hT_hi[:, 4 * half:4 * half + 4, h * P:(h + 1) * P],
                                   psum[:, 4 + b, :].rearrange("p (a b) -> p a b", a=4), ACT.Copy).then_inc(hT_hi_ready[i], 1)

            norm(0, (0, 1))

            def a_gelu(j, h):
                act.wait_ge(ain_biased, 2 * TT * j + 2 * h + 2)
                if j < 2:
                    z = zv[:, h, j * TILE:(j + 1) * TILE]
                    act.activation(z, z, ACT.Gelu, accum_out=v_sum[:, h, j:j + 1]).then_inc(ain_gelu, 1)
                else:
                    z = zu[:, h, (j - 2) * TILE:(j - 1) * TILE]
                    act.activation(z, z, ACT.Gelu).then_inc(ain_gelu, 1)

            for n in range(2, AOUT + 2):
                hi_at(n)
                j, k = (n - 2) // KB - 1, (n - 2) % KB
                if k in (1, 2) and 0 <= j < 3:
                    a_gelu(j, k - 1)
                if n in (2 * KB + 6, 2 * KB + 7):
                    h = n - 2 * KB - 6
                    act.wait_ge(v_centred, h + 1)
                    act.activation(yT_hi[:, 8 * h:8 * h + 8, :].rearrange("p a b -> p (a b)"), zv[:, h, :],
                                   ACT.Square, accum_out=sumsq[:, h:h + 1]).then_inc(v_squares, 1)
                if n == 2 * KB + 9:
                    act.wait_ge(v_ms, 1)
                    act.activation(rms[:, :], meansq[:, :], ACT.Sqrt).then_inc(v_std, 1)
            for h in range(TT):
                a_gelu(3, h)
            for h in range(TT):
                for c in range(4):
                    act.wait_ge(y_turned, 4 * h + c + 1)
                    act.activation(yT_hi[:, 4 * c:4 * c + 4, h * P:(h + 1) * P],
                                   psum[:, 4 * h + c, :].rearrange("p (a b) -> p a b", a=4), ACT.Copy).then_inc(yT_hi_ready, 1)
            for n in range(AOUT + 2, WQ[0] + 1):
                hi_at(n)

            def peer(l):
                norm(1 + 2 * l, (WQ[l] + 1,))
                def copy_scores(g):
                    for h in range(TT):
                        act.wait_ge(scores_done[l], TT * g + h + 1)
                        act.activation(scores[:, h, 4 * g:4 * g + 4, :].rearrange("p a b -> p (a b)"), psum[:, 4 + TT * (g % 2) + h, :],
                                       ACT.Copy).then_inc(scores_copied[l], 1)

                for c in range(N_WQ):
                    hi_at(WQ[l] + 2 + c)
                    act.wait_ge(tile_used, WQ[l] + c + 1)
                    act.activation(qT[:, c, :], psum[:, c % 4, 0:T], ACT.Copy).then_inc(q_copied[l], 1)
                    if c % 4 == 1 and c > 4:
                        copy_scores(c // 4 - 1)
                copy_scores(P_ROWS // 4 - 1)

                def expert_acts(first, last):
                    with act.Fori(first // RAW_SLOTS, last // RAW_SLOTS) as i:
                        for c in range(RAW_SLOTS):
                            hi_in(i, c, UT[l] + 2)
                            act.wait_ge(tile_used, i * RAW_SLOTS + (UT[l] + c + 1))
                            act.activation(acts[:, i * RAW_SLOTS + c, :], psum[:, c, 0:T], ACT.Gelu).then_inc(gelu_done[l], 1)

                act.preload_act_table(ACT.Gelu)
                expert_acts(0, EXP_AT)
                for h in range(TT):
                    act.wait_ge(shifted[l], h + 1)
                    act.activation(picks[:, h, 2, :], picks[:, h, 2, :], ACT.Exp).then_inc(exps[l], 1)
                act.preload_act_table(ACT.Gelu)
                expert_acts(EXP_AT, TURN_AT)
                act.wait_ge(picks_turned[l], 1)
                act.activation(picksT[:, 0:2, :].rearrange("p a b -> p (a b)"), psum[:, 4, :], ACT.Copy).then_inc(picksT_ready[l], 1)
                act.activation(picksT[:, 2, :], psum[:, 5, 0:T], ACT.Copy).then_inc(picksT_ready[l], 1)
                expert_acts(TURN_AT, N_EXP - N_LATE - RAW_SLOTS)

                def gated_onehots(token0, slot, ready, used):
                    act.wait_ge(equal2_ready[l], ready)
                    if used is not None:
                        act.wait_ge(gmat_done[l], used)
                    for c in range(GROUP):
                        ins = act.activation(onehot2[:, slot, c, :], equal2[:, slot, :, c], ACT.Copy,
                                             scale=picksT[:, 2, bass.ds(token0 + c, 1)])
                    ins.then_inc(onehot2_ready[l], 1)

                def late_tile(i, c, more):
                    k = N_EXP - N_LATE + c
                    act.wait_ge(tile_used, i * RAW_SLOTS + (UT[l] + k + 1))
                    if c >= SPLIT_SLOTS or not (isinstance(i, int) and i == 0):
                        act.wait_ge(late_gated[l], i * RAW_SLOTS + (c - 1))
                    act.activation(gelu_out[:, c % 2, :], psum[:, c, 0:T], ACT.Gelu).then_inc(gelu_done[l], 1)
                    hi_in(i, c, UT[l] + 2 + N_EXP - N_LATE)
                    if more:
                        for b in range(2):
                            g = 2 * c + b + 4
                            gated_onehots(i * (8 * GROUP) + g * GROUP, b, i * 8 + (g + 1), i * 8 + (g - 1))

                def gated_hi(k, slot, used):
                    if used is not None:
                        act.wait_ge(tile_used, used)
                    act.activation(w_hi[slot][:, :], acts[:, k, :], ACT.Copy).then_inc(w_hi_ready[l], 1)

                def early_tiles(first, last):
                    for k in range(first, last):
                        hi_at(UT[l] + 2 + k)
                        act.wait_ge(tile_used, UT[l] + k + 1)
                        act.activation(acts[:, k, :], psum[:, k % 4, 0:T], ACT.Gelu).then_inc(gelu_done[l], 1)

                act.wait_ge(picksT_ready[l], 2)
                early = N_EXP - N_LATE
                early_tiles(early - 4, early - 3)
                gated_onehots(0, 0, 1, None)
                early_tiles(early - 3, early - 2)
                gated_onehots(GROUP, 1, 2, None)
                early_tiles(early - 2, early)
                for g in (2, 3):
                    gated_onehots(g * GROUP, g % 2, g + 1, g - 1)
                for c in range(RAW_SLOTS):
                    late_tile(0, c, True)
                with act.Fori(1, N_LATE // RAW_SLOTS - 1) as i:
                    for c in range(RAW_SLOTS):
                        late_tile(i, c, True)
                for c in range(RAW_SLOTS):
                    if c == RAW_SLOTS - 1:
                        act.wait_ge(gated[l], GROUPS)
                        gated_hi(0, 0, None)
                        gated_hi(1, 1, None)
                    late_tile(N_LATE // RAW_SLOTS - 1, c, c < 2)
                act.wait_ge(late_gated[l], N_LATE)
                with act.Fori(0, N_EXP // RAW_SLOTS - 1) as i:
                    for c in range(RAW_SLOTS):
                        gated_hi(i * RAW_SLOTS + (c + 2), c % 2, i * RAW_SLOTS + (VT[l] + c + 1))
                        hi_in(i, c, VT[l] + 2)
                for k in (N_EXP - 2, N_EXP - 1):
                    gated_hi(k, k % 2, VT[l] + k - 1)
                    hi_at(VT[l] + k)

            peer(0)
            hi_at(BQK)
            norm(2, (BQK + 1,))
            act.wait_ge(w_g_loaded, 16)
            act.activation(w_g_hi[:, :, :], w_g[:, :, :], ACT.Copy).then_inc(w_g_hi_ready, 1)
            for n in range(BQK + 2, BRV + 2):
                hi_at(n)
                c = n - 2 - BQK
                act.wait_ge(tile_used, BQK + c + 1)
                if c < B_HEADS:
                    act.activation(gq[:, c, :], psum[:, c % 4, 0:T], ACT.Copy, scale=float(B_HK) ** -0.5).then_inc(qk_copied, 1)
                else:
                    act.activation(gk[:, c - B_HEADS, :], psum[:, c % 4, 0:T], ACT.Copy).then_inc(qk_copied, 1)
                if c == 0:
                    act.wait_ge(glr_done, 1)
                    act.activation(g_lrT[:, :], psum[0:B_RANK, 3, 0:T], ACT.Copy).then_inc(glr_copied, 1)
                if c == 2:
                    act.wait_ge(z_ready, 1)
                    act.activation(z_tmp[:, :, :], z_la[:, :, :], ACT.Abs).then_inc(la_abs, 1)
                if c == 3:
                    act.wait_ge(la_abs, 1)
                    act.activation(z_tmp[:, :, :], z_tmp[:, :, :], ACT.Exp, scale=-1.0).then_inc(la_exp, 1)
                if c == 4:
                    act.wait_ge(la_exp, 1)
                    act.activation(z_tmp[:, :, :], z_tmp[:, :, :], ACT.Ln, bias=1.0).then_inc(la_ln, 1)
            act.wait_ge(gcum_done, 1)
            act.activation(gcum[:, :, :].rearrange("p a b -> p (a b)"), bank_pair(6), ACT.Copy).then_inc(gcum_copied, 1)

            def decay(L):
                act.wait_ge(diff_ready, L)
                if L == 1:
                    act.activation(ed[1][:, :, 0:P], ed[1][:, :, 0:P], ACT.Exp)
                    act.activation(ed[1][:, :, P:T], gcum[:, :, P:T], ACT.Exp).then_inc(decay_ready, 1)
                    return
                act.activation(ed[L % 2][:, :, :], ed[L % 2][:, :, :], ACT.Exp).then_inc(decay_ready, 1)

            act.wait_ge(gcum_copied, 1)
            decay(1)
            for n in range(BRV + 2, BOUT + 2):
                c = n - 2 - BRV
                if c not in (KB - 1, 2 * KB - 1):
                    hi_at(n)
                if c < 2:
                    decay(c + 2)
                elif c % 2 == 0 and c // 2 + 3 <= B_LEVELS + 1:
                    decay(c // 2 + 3)
                if c in (KB - 1, 2 * KB - 1):
                    dst, copied = (br, br_copied) if c == KB - 1 else (bv, bv_copied)
                    act.wait_ge(tile_used, BRV + c + 1)
                    for b in range(4):
                        act.activation(dst[:, b // 2, (b % 2) * BANK:(b % 2 + 1) * BANK], psum[:, b, :], ACT.Copy).then_inc(copied, 1)
                    hi_at(n)
                if c == KB + 5:
                    act.wait_ge(br_copied, 4)
                    act.activation(bsg[:, :, :], br[:, :, :], ACT.Sigmoid).then_inc(sig_done, 1)
            act.preload_act_table(ACT.Sqrt)
            for h in range(TT):
                act.wait_ge(o_done, h + 1)
                for d in range(B_HEADS):
                    ins = act.activation(qe[h][:, d, :], psum[:, 2 * h + d // 2, (d % 2) * B_HV:(d % 2 + 1) * B_HV],
                                         ACT.Square, accum_out=head_ms[:, h, 0, d:d + 1])
                ins.then_inc(o_squares, 1)
                act.wait_ge(o_ms, h + 1)
                act.activation(head_ms[:, h, 2, :], head_ms[:, h, 1, :], ACT.Sqrt).then_inc(o_rms, 1)
            for b in range(2 * TT):
                h, half = b // 2, b % 2
                act.wait_ge(o_turned, b + 1)
                act.activation(hT_hi[:, 4 * half:4 * half + 4, h * P:(h + 1) * P],
                               psum[:, 4 + b, :].rearrange("p (a b) -> p a b", a=4), ACT.Copy).then_inc(oT_hi_ready, 1)
            for n in range(BOUT + 2, WQ[1] + 1):
                hi_at(n)
            peer(1)
            norm(4, ())

        @block.vector
        def _(dve):
            def lo(slot, ready):
                dve.wait_ge(hi_ready, ready)
                s = slot % SPLIT_SLOTS
                dve.tensor_tensor(tile_lo[s][:, :], raw[slot][:, :], tile_hi[s][:, :].bitcast(F32),
                                  ALU.subtract).then_inc(lo_ready, 1)

            def lo_at(n):
                lo(n % RAW_SLOTS, n + 1)

            def lo_in(i, c, first):
                lo((first + c) % RAW_SLOTS, i * RAW_SLOTS + (first + c + 1))

            chain = [0]

            def did(ins):
                ins.then_inc(dve_chain, 1)
                chain[0] += 1
                return chain[0]

            def after(number):
                dve.wait_ge(dve_chain, number)

            def norm(i, n=None):
                for h in range(TT):
                    dve.wait_ge(squares[i], h + 1)
                    dve.tensor_scalar(meansq[:, h:h + 1], sumsq[:, h:h + 1], 1.0 / D, EPS, ALU.mult, ALU.add).then_inc(ms_ready[i], 1)
                    dve.wait_ge(rms_ready[i], h + 1)
                    after(did(dve.reciprocal(rstd[:, h:h + 1], rms[:, h:h + 1])))
                    dve.wait_ge(gain_loaded[i], 16)
                    if i == 0:
                        dve.wait_ge(x_loaded[h], 16)
                    for half in range(2):
                        cols = slice(half * BANK, (half + 1) * BANK)
                        dve.scalar_tensor_tensor(hn[:, h, cols], x[:, h, cols], rstd[:, h:h + 1], gain_row[:, cols],
                                                 ALU.mult, ALU.mult).then_inc(hn_ready[i], 1)
                if i == 4:
                    return
                lo_at(n)
                for b in range(2 * TT):
                    h, half = b // 2, b % 2
                    dve.wait_ge(hT_hi_ready[i], b + 1)
                    place = (slice(None), slice(4 * half, 4 * half + 4), slice(h * P, (h + 1) * P))
                    dve.tensor_tensor(hT_lo[place], psum[:, 4 + b, :].rearrange("p (a b) -> p a b", a=4),
                                      hT_hi[place].bitcast(F32), ALU.subtract).then_inc(hT_lo_ready[i], 1)
                lo_at(n + 1)

            def add_to_x(i, first_bank, last_tile):
                for b in range(4):
                    if b == 0:
                        dve.wait_ge(half_done[i], 1)
                    if b == 2:
                        dve.wait_ge(tile_used, last_tile + 1)
                    part = x[:, b // 2, (b % 2) * BANK:(b % 2 + 1) * BANK]
                    dve.tensor_tensor(part, psum[:, first_bank + b, :], part, ALU.add).then_inc(x_ready[i], 1)

            norm(0, 0)
            dve.wait_ge(consts_loaded, 16)
            dve.tensor_copy(numbers16[:, :, :], iota.unsqueeze(2).broadcast_to([P, P, GROUP])).then_inc(numbers_ready, 1)

            def a_bias(j):
                dve.wait_ge(tile_used, (j + 1) * KB)
                dve.wait_ge(b_in_loaded[j // 2], 16)
                for b in range(4):
                    h, cols = b // 2, (j % 2) * TILE + (b % 2) * BANK
                    z = zv if j < 2 else zu
                    dve.tensor_tensor(z[:, h, cols:cols + BANK], psum[:, 4 * (j % 2) + b, :],
                                      b_in[:, j * TILE + (b % 2) * BANK:j * TILE + (b % 2 + 1) * BANK], ALU.add).then_inc(ain_biased, 1)

            for n in range(2, AOUT + 2):
                if n == AOUT + 1:
                    a_bias(A_BLOCKS - 1)
                lo_at(n)
                if (n - 1) % KB == 0 and KB < n < AOUT:
                    a_bias((n - 1) // KB - 1)
                step = n - 2 * KB
                if step == 4:
                    dve.wait_ge(ain_gelu, 4)
                    after(did(dve.tensor_tensor(v_mean[:, :], v_sum[:, :, 0], v_sum[:, :, 1], ALU.add)))
                    after(did(dve.tensor_scalar(v_mean[:, :], v_mean[:, :], 1.0 / A_WIDTH, None, ALU.mult)))
                if step in (5, 6):
                    h = step - 5
                    dve.tensor_scalar(zv[:, h, :], zv[:, h, :], v_mean[:, h:h + 1], None, ALU.subtract).then_inc(v_centred, 1)
                if step == 9:
                    dve.wait_ge(v_squares, TT)
                    dve.tensor_scalar(meansq[:, :], sumsq[:, :], 1.0 / A_WIDTH, EPS, ALU.mult, ALU.add).then_inc(v_ms, 1)
                if step == 10:
                    dve.wait_ge(v_std, 1)
                    dve.wait_ge(small_loaded, 16 * N_SMALL)
                    after(did(dve.reciprocal(rstd[:, :], rms[:, :])))
                if step in (11, 12, 13, 14):
                    h, cols = (step - 11) // 2, slice((step - 11) % 2 * TILE, (step - 11) % 2 * TILE + TILE)
                    dve.scalar_tensor_tensor(zv[:, h, cols], zv[:, h, cols], rstd[:, h:h + 1], ln_g[:, cols],
                                             ALU.mult, ALU.mult).then_inc(v_scaled, 1)
            for h in range(TT):
                dve.wait_ge(ain_gelu, 7 + h)
                dve.wait_ge(sv_done, h + 1)
                for g in range(A_GROUPS):
                    u = zu[:, h, g * A_GDIM:(g + 1) * A_GDIM]
                    bank, col = 4 * h + g // 2, (g % 2) * A_GDIM
                    dve.scalar_tensor_tensor(u, psum[:, bank, col:col + A_GDIM], b_sT[:, g:g + 1], u,
                                             ALU.add, ALU.mult).then_inc(y_ready, 1)
            for h in range(TT):
                for c in range(4):
                    dve.wait_ge(yT_hi_ready, 4 * h + c + 1)
                    dst = (slice(None), slice(4 * c, 4 * c + 4), slice(h * P, (h + 1) * P))
                    dve.tensor_tensor(yT_lo[dst], psum[:, 4 * h + c, :].rearrange("p (a b) -> p a b", a=4),
                                      yT_hi[dst].bitcast(F32), ALU.subtract).then_inc(yT_lo_ready, 1)
            for n in range(AOUT + 2, WQ[0]):
                lo_at(n)
            add_to_x(1, 0, WQ[0] - 1)

            def top16(rows, values, places, between):
                n8 = [did(dve.max(values[r][:, 0:8], rows[r])) for r in range(2)]
                for r in range(2):
                    after(n8[r])
                    n8[r] = did(dve.max_index(places[r][:, 0:8], values[r][:, 0:8], rows[r]))
                if between:
                    between[0]()
                for r in range(2):
                    after(n8[r])
                    n8[r] = did(dve.match_replace(rows[r], values[r][:, 0:8], rows[r], LOWEST))
                for r in range(2):
                    after(n8[r])
                    n8[r] = did(dve.max(values[r][:, 8:16], rows[r]))
                if len(between) > 1:
                    between[1]()
                for r in range(2):
                    after(n8[r])
                    n8[r] = did(dve.max_index(places[r][:, 8:16], values[r][:, 8:16], rows[r]))
                return n8[1]

            def two_tiles(n):
                lo_at(n)
                lo_at(n + 1)
                return n + 2

            def peer(l):
                norm(1 + 2 * l, WQ[l])
                for n in range(WQ[l] + 2, WQ[l] + 8):
                    lo_at(n)
                n = WQ[l] + 8
                for g in range(P_ROWS // 4):
                    for h in range(TT):
                        dve.wait_ge(scores_copied[l], TT * g + h + 1)
                        for r in (4 * g, 4 * g + 2):
                            lo_at(n)
                            top16([scores[:, h, r + k, :] for k in range(2)], [topv[:, h, r + k, :] for k in range(2)],
                                  [topi[:, h, r + k, :] for k in range(2)], [lambda: lo_at(n + 1)])
                            n += 2
                for h in range(TT):
                    lo_at(n)
                    n += 1
                    after(chain[0])
                    v1 = topv[:, h, 0:P_ROWS:2, :].unsqueeze(3).broadcast_to([P, P_HEADS, TOPK, TOPK])
                    v2 = topv[:, h, 1:P_ROWS:2, :].unsqueeze(2).broadcast_to([P, P_HEADS, TOPK, TOPK])
                    sums = did(dve.tensor_tensor(cand[:, :, :].rearrange("p g (a b) -> p g a b", a=TOPK), v1, v2, ALU.add))
                    lo_at(n)
                    n += 1
                    after(sums)
                    for g in range(0, P_HEADS, 2):
                        lo_at(n)
                        top16([cand[:, g + k, :] for k in range(2)], [candv[:, g + k, :] for k in range(2)],
                              [candpos[:, g + k, :] for k in range(2)], [lambda: lo_at(n + 1), lambda: lo_at(n + 2)])
                        n += 3
                    lo_at(n)
                    n += 1
                    after(chain[0])
                    a1 = did(dve.tensor_scalar(pos_a[:, :, :], candpos[:, :, :], 4, None, ALU.logical_shift_right))
                    a2 = did(dve.tensor_scalar(pos_b[:, :, :], candpos[:, :, :], 15, None, ALU.bitwise_and))
                    a3 = did(dve.tensor_copy(topi_f[:, :, :], topi[:, h, :, :]))
                    after(a1)
                    a1 = did(dve.tensor_copy(pos_af[:, :, :], pos_a[:, :, :]))
                    after(a2)
                    a2 = did(dve.tensor_copy(pos_bf[:, :, :], pos_b[:, :, :]))
                    after(a3)
                    for half, pos in ((0, pos_af), (1, pos_bf)):
                        after((a1, a2)[half])
                        want = pos[:, :, :].unsqueeze(3).broadcast_to([P, P_HEADS, TOPK, TOPK])
                        ranks = iota[:, 0:TOPK].unsqueeze(1).unsqueeze(1).broadcast_to([P, P_HEADS, TOPK, TOPK])
                        numbers = topi_f[:, half:P_ROWS:2, :].unsqueeze(2).broadcast_to([P, P_HEADS, TOPK, TOPK])
                        n = two_tiles(n)
                        eq = did(dve.tensor_tensor(look[:, :, :, :], want, ranks, ALU.is_equal))
                        n = two_tiles(n)
                        after(eq)
                        eq = did(dve.tensor_tensor(look[:, :, :, :], look[:, :, :, :], numbers, ALU.mult))
                        n = two_tiles(n)
                        after(eq)
                        eq = did(dve.tensor_reduce(picks[:, h, half, :].rearrange("p (g k) -> p g k", g=P_HEADS),
                                                   look[:, :, :, :], AX.X, ALU.add))
                        after(eq)
                    dve.tensor_tensor(picks[:, h, 2, :].rearrange("p (g k) -> p g k", g=P_HEADS), candv[:, :, :],
                                      candv[:, :, 0:1].broadcast_to([P, P_HEADS, TOPK]), ALU.subtract).then_inc(shifted[l], 1)
                    dve.wait_ge(shifted[l], h + 1)
                assert n <= UT[l] + 2 + EXP_AT, n - UT[l]
                while n < UT[l] + 2 + EXP_AT:
                    lo_at(n)
                    n += 1
                for h in range(TT):
                    e = picks[:, h, 2, :].rearrange("p (g k) -> p g k", g=P_HEADS)
                    dve.wait_ge(exps[l], h + 1)
                    after(did(dve.tensor_reduce(head_sum[:, h, :], e, AX.X, ALU.add)))
                    after(did(dve.reciprocal(head_inv[:, h, :], head_sum[:, h, :])))
                    dve.tensor_tensor(e, e, head_inv[:, h, :].unsqueeze(2).broadcast_to([P, P_HEADS, TOPK]),
                                      ALU.mult).then_inc(gates_ready[l], 1)
                first_onehots = N_EXP - N_LATE - RAW_SLOTS
                with dve.Fori(0, (first_onehots - EXP_AT) // RAW_SLOTS) as i:
                    for c in range(RAW_SLOTS):
                        lo_in(i, c, UT[l] + 2 + EXP_AT)

                def onehot(token0, slot):
                    rows = iota.unsqueeze(1).broadcast_to([P, GROUP, P])
                    number = picksT[:, 0, bass.ds(token0, GROUP)].unsqueeze(2).broadcast_to([P, GROUP, P])
                    dve.tensor_tensor(onehot1[:, slot, :, :], rows, number, ALU.is_equal).then_inc(onehot1_ready[l], 1)

                def gate(token0, c, done):
                    dve.wait_ge(gmat_done[l], done)
                    a = acts[:, :, bass.ds(token0, GROUP)].rearrange("p i t -> p t i")
                    dve.tensor_tensor(a, psum[:, 4 + c % 4, :].rearrange("p (t i) -> p t i", t=GROUP), a, ALU.mult).then_inc(gated[l], 1)

                def equal(token0, slot, read):
                    if read is not None:
                        dve.wait_ge(onehot2_ready[l], read)
                    number = picks16[:, bass.ds(token0, GROUP)].unsqueeze(1).broadcast_to([P, P, GROUP])
                    dve.tensor_tensor(equal2[:, slot, :, :], numbers16[:, :, :], number, ALU.is_equal).then_inc(equal2_ready[l], 1)

                def gated_lo(k, slot, ready):
                    dve.wait_ge(w_hi_ready[l], ready)
                    dve.tensor_tensor(w_lo[slot][:, :], acts[:, k, :], w_hi[slot][:, :].bitcast(F32), ALU.subtract).then_inc(w_lo_ready[l], 1)

                def late_tile(i, c):
                    last = isinstance(i, int)
                    for b in range(2):
                        g = 2 * c + b
                        gate(i * (8 * GROUP) + g * GROUP, g, i * 8 + (g + 1))
                        if not (last and g + 2 >= 8):
                            onehot(i * (8 * GROUP) + (g + 2) * GROUP, b)
                    for b in range(2):
                        g = 2 * c + b
                        if not (last and g + 4 >= 8):
                            equal(i * (8 * GROUP) + (g + 4) * GROUP, b, i * 8 + (g + 3))
                    dve.wait_ge(gated[l], i * 8 + (2 * c + 2))
                    if last and c == RAW_SLOTS - 1:
                        gated_lo(0, 0, 1)
                        lo_at(VT[l])
                    dve.wait_ge(gelu_done[l], i * RAW_SLOTS + (N_EXP - N_LATE + c + 1))
                    place = acts[:, i * RAW_SLOTS + (N_EXP - N_LATE + c), :]
                    dve.tensor_tensor(place, place, gelu_out[:, c % 2, :], ALU.mult).then_inc(late_gated[l], 1)
                    dve.wait_ge(late_gated[l], i * RAW_SLOTS + (c + 1))

                dve.wait_ge(picksT_ready[l], 2)
                turned = did(dve.tensor_copy(picks16[:, :], picksT[:, 1, :]))
                onehot(0, 0)
                onehot(GROUP, 1)
                after(turned)
                dve.wait_ge(numbers_ready, 1)
                for g in range(4):
                    equal(g * GROUP, g % 2, g - 1 if g >= 2 else None)
                    if g == 1:
                        for k in range(first_onehots + 2, N_EXP - N_LATE):
                            lo_at(UT[l] + k)
                dve.wait_ge(ones_ready[l], 1)
                dve.wait_ge(gelu_done[l], N_EXP - N_LATE)
                with dve.Fori(0, N_LATE // RAW_SLOTS - 1) as i:
                    for c in range(RAW_SLOTS):
                        late_tile(i, c)
                for c in range(RAW_SLOTS):
                    late_tile(N_LATE // RAW_SLOTS - 1, c)
                gated_lo(1, 1, 2)
                lo_at(VT[l] + 1)
                with dve.Fori(0, N_EXP // RAW_SLOTS - 1) as i:
                    for c in range(RAW_SLOTS):
                        gated_lo(i * RAW_SLOTS + (c + 2), c % 2, i * RAW_SLOTS + (c + 3))
                        lo_in(i, c, VT[l] + 2)
                for k in (N_EXP - 2, N_EXP - 1):
                    gated_lo(k, k % 2, k + 1)
                    lo_at(VT[l] + k)

            peer(0)
            add_to_x(2, 4, BQK - 1)
            norm(2, BQK)
            dve.wait_ge(w_g_hi_ready, 1)
            dve.tensor_tensor(w_g_lo[:, :, :], w_g[:, :, :], w_g_hi[:, :, :].bitcast(F32), ALU.subtract).then_inc(w_g_lo_ready, 1)
            for n in range(BQK + 2, BRV + 2):
                lo_at(n)
                c = n - 2 - BQK
                if c == 1:
                    dve.wait_ge(la_done, TT)
                    dve.wait_ge(gla_loaded, 16 * 4)
                    dve.tensor_tensor(z_la[:, :, :], psum[:, 5:7, :], bg_row[:, :].unsqueeze(1).broadcast_to([P, TT, B_KEY]),
                                      ALU.add).then_inc(z_ready, 1)
                if c == 5:
                    dve.wait_ge(la_ln, 1)
                    dve.scalar_tensor_tensor(z_la[:, :, :].rearrange("p a b -> p (a b)"), z_la[:, :, :].rearrange("p a b -> p (a b)"), 0.0,
                                             z_tmp[:, :, :].rearrange("p a b -> p (a b)"), ALU.min, ALU.subtract).then_inc(la_ready, 1)

            def decayed(L):
                dve.wait_ge(decay_ready, L)
                if L >= 3:
                    dve.wait_ge(level_done, L - 1)
                dve.tensor_tensor(qe[L % 2][:, :, :], gq[:, :, :], ed[L % 2][:, :, :], ALU.mult)
                dve.tensor_tensor(ke[L % 2][:, :, :], gk[:, :, :], ed[L % 2][:, :, :], ALU.mult).then_inc(qk_decayed, 1)

            def keep(L):
                dve.wait_ge(level_done, L + 1)
                if L > 0:
                    dve.wait_ge(level_kept, L)
                if L == 1:
                    dve.tensor_copy(score_x[:, :, :].rearrange("p a b -> p (a b)"), psum[:, 6, :]).then_inc(level_kept, 1)
                    return
                mask = masks[:, B_LEVELS if L == 0 else L - 2, :].unsqueeze(1).broadcast_to([P, B_HEADS * TT, P])
                dve.copy_predicated(score_in[:, :, :], mask,
                                    bank_pair(4 + 2 * (L % 2)).rearrange("p (a b) -> p a b", b=P)).then_inc(level_kept, 1)

            dve.wait_ge(gla_loaded, 16 * 4)
            dve.wait_ge(score_zeroed, 1)
            dve.wait_ge(qk_copied, 2 * B_HEADS)
            decayed(1)
            levels = B_LEVELS + 2
            for n in range(BRV + 2, BOUT + 2):
                c = n - 2 - BRV
                if c < 2 * KB - 1:
                    lo_at(n)
                if c % 2 == 0 and c // 2 + 2 < levels:
                    decayed(c // 2 + 2)
                if c % 2 == 1:
                    keep(c // 2)
            keep(levels - 1)
            lo_at(BOUT + 1)
            for h in range(TT):
                dve.wait_ge(br_normed, h + 1)
                dve.wait_ge(sig_done, 1)
                dve.tensor_tensor(br[:, h, :], bo[:, h, :], bsg[:, h, :], ALU.mult).then_inc(silu_done, 1)
            dve.wait_ge(silu_done, TT)
            for h in range(TT):
                dve.wait_ge(o_squares, h + 1)
                dve.tensor_scalar(head_ms[:, h, 1, :], head_ms[:, h, 0, :], 1.0 / B_HV, EPS, ALU.mult, ALU.add).then_inc(o_ms, 1)
                dve.wait_ge(o_rms, h + 1)
                after(did(dve.reciprocal(head_ms[:, h, 3, :], head_ms[:, h, 2, :])))
                for d in range(B_HEADS):
                    cols = slice(d * B_HV, (d + 1) * B_HV)
                    dve.scalar_tensor_tensor(bo[:, h, cols], psum[:, 2 * h + d // 2, (d % 2) * B_HV:(d % 2 + 1) * B_HV],
                                             head_ms[:, h, 3, d:d + 1], br[:, h, cols], ALU.mult, ALU.mult).then_inc(o_ready, 1)
            for b in range(2 * TT):
                h, half = b // 2, b % 2
                dve.wait_ge(oT_hi_ready, b + 1)
                place = (slice(None), slice(4 * half, 4 * half + 4), slice(h * P, (h + 1) * P))
                dve.tensor_tensor(hT_lo[place], psum[:, 4 + b, :].rearrange("p (a b) -> p a b", a=4),
                                  hT_hi[place].bitcast(F32), ALU.subtract).then_inc(oT_lo_ready, 1)
            for n in range(BOUT + 2, WQ[1]):
                lo_at(n)
            add_to_x(3, 0, WQ[1] - 1)
            peer(1)
            add_to_x(4, 4, TILES - 1)
            norm(4)

        @block.tensor
        def _(pe):
            def product(o, a, b, start=False, stop=False):
                return pe.matmul(o, a, b, start=start, stop=stop, skip_group_check=True)

            def stationary_tile(slot, ready, bank, rest_ready, hT_hi_wait=None, hT_lo_wait=None):
                w_h, w_l = tile_hi[slot], tile_lo[slot]
                o = psum[:, bank, 0:T]
                pe.wait_ge(hi_ready, ready)
                for kb in range(KB):
                    if kb == KB // 2 and hT_hi_wait is not None:
                        pe.wait_ge(*hT_hi_wait)
                    w = w_h[:, kb * P:(kb + 1) * P]
                    product(o, w, hT_hi[:, kb, :], start=kb == 0)
                    if hT_lo_wait is None:
                        product(o, w, hT_lo[:, kb, :])
                if hT_lo_wait is not None:
                    pe.wait_ge(*hT_lo_wait)
                    for kb in range(KB):
                        product(o, w_h[:, kb * P:(kb + 1) * P], hT_lo[:, kb, :])
                pe.wait_ge(*rest_ready)
                for kb in range(KB):
                    ins = product(o, w_l[:, kb * P:(kb + 1) * P], hT_hi[:, kb, :], stop=kb == KB - 1)
                ins.then_inc(tile_used, 1)

            def moving_tile(slot, ready, rest_ready, first_bank, a_hi, a_lo, start, stop, a_lo_ready=None, half=None, bank_free=None):
                pe.wait_ge(hi_ready, ready)
                if half is not None:
                    pe.wait_ge(*(a_lo_ready or (hi_ready, ready)))
                    for h in range(TT):
                        cols = slice(h * P, (h + 1) * P)
                        for a, w in ((a_hi, tile_hi), (a_lo, tile_hi), (a_hi, tile_lo)):
                            if w is tile_lo:
                                pe.wait_ge(lo_ready, rest_ready)
                            for d in range(2):
                                ins = product(psum[:, first_bank + 2 * h + d, :], a[:, cols], w[slot][:, d * BANK:(d + 1) * BANK],
                                              stop=w is tile_lo)
                        ins.then_inc(half if h == 0 else tile_used, 1)
                    return
                for a, first in ((a_hi, start), (a_lo, False)):
                    if a is a_lo and a_lo_ready is not None:
                        pe.wait_ge(*a_lo_ready)
                    for h in range(TT):
                        cols = slice(h * P, (h + 1) * P)
                        for d in range(2):
                            if bank_free is not None and a is a_hi:
                                pe.wait_ge(bank_free[0], bank_free[1] + 2 * h + d + 1)
                            product(psum[:, first_bank + 2 * h + d, :], a[:, cols], tile_hi[slot][:, d * BANK:(d + 1) * BANK], start=first)
                pe.wait_ge(lo_ready, rest_ready)
                for h in range(TT):
                    cols = slice(h * P, (h + 1) * P)
                    for d in range(2):
                        ins = product(psum[:, first_bank + 2 * h + d, :], a_hi[:, cols], tile_lo[slot][:, d * BANK:(d + 1) * BANK], stop=stop)
                ins.then_inc(tile_used, 1)

            def turn(src, first_bank, blocks):
                for b in range(blocks):
                    ins = pe.transpose(psum[:, first_bank + b // 4, (b % 4) * P:(b % 4 + 1) * P], src[:, b * P:(b + 1) * P], ident)
                return ins

            def norm(i):
                for h in range(TT):
                    for half in range(2):
                        pe.wait_ge(hn_ready[i], 2 * h + half + 1)
                        turn(hn[:, h, half * BANK:(half + 1) * BANK], 4 + 2 * h + half, KB // 2).then_inc(hn_turned[i], 1)
                pe.wait_ge(hT_hi_ready[i], 2 * TT - 1)

            pe.wait_ge(consts_loaded, 16)
            norm(0)
            for j in range(A_BLOCKS):
                if j >= 2:
                    pe.wait_ge(ain_biased, 4 * (j - 1))
                for kb in range(KB):
                    n = AIN + j * KB + kb
                    if n == KB // 2:
                        pe.wait_ge(hT_hi_ready[0], 2 * TT)
                    moving_tile(n % 2, n + 1, lo_count(n), 4 * (j % 2), hT_hi[:, kb, :], hT_lo[:, kb, :], kb == 0, kb == KB - 1,
                                (hT_lo_ready[0], 2 * TT) if n == AIN else None)
            pe.wait_ge(ws_masked, 1)
            for h in range(TT):
                pe.wait_ge(v_normed, 2 * h + 2)
                pe.wait_ge(ain_biased, 4 * (3 + h))
                for g in range(A_GROUPS):
                    ins = product(psum[:, 4 * h + g // 2, (g % 2) * A_GDIM:(g % 2 + 1) * A_GDIM], wsT[:, g, :],
                                  zv[:, h, g * A_GDIM:(g + 1) * A_GDIM], start=True, stop=True)
                ins.then_inc(sv_done, 1)
            for h in range(TT):
                for c in range(4):
                    pe.wait_ge(y_ready, A_GROUPS * h + 2 * c + 2)
                    turn(zu[:, h, c * BANK:(c + 1) * BANK], 4 * h + c, 4).then_inc(y_turned, 1)
            pe.wait_ge(yT_lo_ready, 4)
            for kb in range(YB):
                n = AOUT + kb
                if kb % 4 == 0:
                    pe.wait_ge(yT_hi_ready, 5 + kb // 4)
                moving_tile(n % 2, n + 1, lo_count(n), 0, yT_hi[:, kb, :], yT_lo[:, kb, :], kb == 0, kb == YB - 1,
                            (yT_lo_ready, 5 + kb // 4) if kb % 4 == 0 else None, half=half_done[1] if kb == YB - 1 else None)

            def peer(l):
                norm(1 + 2 * l)
                def row_scores(r):
                    pe.wait_ge(q_copied[l], r + 1)
                    if r % 4 == 0 and r >= 8:
                        pe.wait_ge(scores_copied[l], TT * (r // 4 - 1))
                    for h in range(TT):
                        ins = product(psum[:, 4 + TT * (r // 4 % 2) + h, (r % 4) * NK:(r % 4 + 1) * NK], qT[:, r, h * P:(h + 1) * P],
                                      keysT[:, l, r % 2, :], start=True, stop=True)
                        if r % 4 == 3:
                            ins.then_inc(scores_done[l], 1)

                for c in range(N_WQ):
                    n = WQ[l] + c
                    if c >= 4:
                        pe.wait_ge(q_copied[l], c - 3)
                    stationary_tile(n % 2, n + 1, c % 4, (lo_ready, lo_count(n)), *(((hT_hi_ready[1 + 2 * l], 2 * TT), (hT_lo_ready[1 + 2 * l], 2 * TT)) if c == 0 else ()))
                    if c == 0:
                        pe.wait_ge(small_loaded, 16 * N_SMALL)
                        pe.wait_ge(hT_lo_ready[1 + 2 * l], 2 * TT)
                    if c > 0:
                        row_scores(c - 1)
                for c in range(RAW_SLOTS):
                    pe.wait_ge(q_copied[l], N_WQ - 3 + c)
                    stationary_tile(c % 2, UT[l] + c + 1, c, (lo_ready, lo_count(UT[l] + c)))
                    if c == 0:
                        row_scores(N_WQ - 1)

                def expert_tile(i, c, rest=None):
                    pe.wait_ge(gelu_done[l], i * RAW_SLOTS + (c + 1 - RAW_SLOTS))
                    stationary_tile(c % 2, i * RAW_SLOTS + (UT[l] + c + 1), c,
                                    rest or (lo_ready, i * RAW_SLOTS + lo_count(UT[l] + c)))

                with pe.Fori(1, TURN_AT // RAW_SLOTS) as i:
                    for c in range(RAW_SLOTS):
                        expert_tile(i, c)
                pe.wait_ge(scores_copied[l], 4 * TT)
                pe.wait_ge(gates_ready[l], TT)
                for k in range(3):
                    for h in range(TT):
                        c = 2 * k + h
                        ins = pe.transpose(psum[:, 4 + c // 4, (c % 4) * P:(c % 4 + 1) * P], picks[:, h, k, :], ident)
                ins.then_inc(picks_turned[l], 1)
                with pe.Fori(TURN_AT // RAW_SLOTS, (N_EXP - N_LATE) // RAW_SLOTS) as i:
                    for c in range(RAW_SLOTS):
                        expert_tile(i, c)

                def gate_matrices(g, ready, bank_out):
                    pe.wait_ge(onehot1_ready[l], ready)
                    pe.wait_ge(onehot2_ready[l], ready)
                    if bank_out is not None:
                        pe.wait_ge(gated[l], bank_out)
                    for c in range(GROUP):
                        ins = product(psum[:, 4 + g % 4, c * P:(c + 1) * P], onehot1[:, g % 2, c, :], onehot2[:, g % 2, c, :],
                                      start=True, stop=True)
                    ins.then_inc(gmat_done[l], 1)

                pe.wait_ge(picksT_ready[l], 2)
                for c in range(RAW_SLOTS):
                    for g in (2 * c, 2 * c + 1):
                        gate_matrices(g, g + 1, g - 3 if g >= 4 else None)
                    expert_tile((N_EXP - N_LATE) // RAW_SLOTS, c, (late_lo_ready[l], c + 1))
                with pe.Fori(1, N_LATE // RAW_SLOTS) as i:
                    for c in range(RAW_SLOTS):
                        for g in (2 * c, 2 * c + 1):
                            gate_matrices(g, i * 8 + (g + 1), i * 8 + (g - 3))
                        expert_tile(i + (N_EXP - N_LATE) // RAW_SLOTS, c, (late_lo_ready[l], i * RAW_SLOTS + (c + 1)))

                def value_tile(slot, ready, rest_ready, k, start, stop, half=None):
                    pe.wait_ge(w_hi_ready[l], k + 1)
                    moving_tile(slot, ready, rest_ready, 4, w_hi[slot], w_lo[slot], start, stop, (w_lo_ready[l], k + 1), half)

                for k in range(RAW_SLOTS):
                    value_tile(k % 2, VT[l] + k + 1, lo_count(VT[l] + k), k, k == 0, False)
                with pe.Fori(1, N_EXP // RAW_SLOTS - 1) as i:
                    for c in range(RAW_SLOTS):
                        value_tile(c % 2, i * RAW_SLOTS + (VT[l] + c + 1), i * RAW_SLOTS + lo_count(VT[l] + c), i * RAW_SLOTS + c, False, False)
                for k in range(N_EXP - RAW_SLOTS, N_EXP):
                    value_tile(k % 2, VT[l] + k + 1, lo_count(VT[l] + k), k, False, k == N_EXP - 1,
                               half_done[2 + 2 * l] if k == N_EXP - 1 else None)

            peer(0)
            norm(2)
            for c in range(N_BQK):
                n = BQK + c
                if c >= 4:
                    pe.wait_ge(qk_copied, c - 3)
                stationary_tile(n % 2, n + 1, c % 4, (lo_ready, lo_count(n)), *(((hT_hi_ready[2], 2 * TT), (hT_lo_ready[2], 2 * TT)) if c == 0 else ()))
                if c == 0:
                    pe.wait_ge(w_g_hi_ready, 1)
                    for kb in range(KB):
                        product(psum[0:B_RANK, 3, 0:T], w_g_hi[:, kb, :], hT_hi[:, kb, :], start=kb == 0)
                    pe.wait_ge(w_g_lo_ready, 1)
                    pe.wait_ge(hT_lo_ready[2], 2 * TT)
                    for kb in range(KB):
                        product(psum[0:B_RANK, 3, 0:T], w_g_lo[:, kb, :], hT_hi[:, kb, :])
                        ins = product(psum[0:B_RANK, 3, 0:T], w_g_hi[:, kb, :], hT_lo[:, kb, :], stop=kb == KB - 1)
                    ins.then_inc(glr_done, 1)
                    pe.wait_ge(gla_loaded, 16 * 4)
                if c == 1:
                    pe.wait_ge(glr_copied, 1)
                    for h in range(TT):
                        product(psum[:, 5 + h, :], g_lrT[:, h * P:(h + 1) * P], w_g2[:, :], start=True, stop=True).then_inc(la_done, 1)
                if c == 7:
                    pe.wait_ge(la_ready, 1)
                    for d in range(B_HEADS):
                        for h in range(TT):
                            ins = product(psum[:, 6 + d // 2, (d % 2) * T + h * P:(d % 2) * T + (h + 1) * P],
                                          z_la[:, h, d * B_HK:(d + 1) * B_HK], tri16, start=True, stop=True)
                    ins.then_inc(gcum_done, 1)

            def level(L):
                q, k = (gq, gk) if L == 0 else (qe[L % 2], ke[L % 2])
                if L == 0:
                    pe.wait_ge(qk_copied, 2 * B_HEADS)
                else:
                    pe.wait_ge(qk_decayed, L)
                if L == 1:
                    pe.wait_ge(gcum_copied, 1)
                if L >= 2:
                    pe.wait_ge(level_kept, L - 1)
                first = 4 + 2 * (L % 2)
                for d in range(B_HEADS):
                    if L == 1:
                        ins = product(psum[:, first, d * P:(d + 1) * P], k[:, d, 0:P], q[:, d, P:T], start=True, stop=True)
                        continue
                    for h in range(TT):
                        c = TT * d + h
                        ins = product(psum[:, first + c // 4, (c % 4) * P:(c % 4 + 1) * P], k[:, d, h * P:(h + 1) * P],
                                      q[:, d, h * P:(h + 1) * P], start=True, stop=True)
                ins.then_inc(level_done, 1)

            for c in range(N_BRV):
                n = BRV + c
                kb = c % KB
                moving_tile(n % 2, n + 1, lo_count(n), 0, hT_hi[:, kb, :], hT_lo[:, kb, :], kb == 0, kb == KB - 1,
                            bank_free={0: (qk_copied, 4), KB: (br_copied, 0)}.get(c))
                if c == 0:
                    level(0)
                elif (c % 2 == 0 and c != KB) or c == KB - 1:
                    level((c + 1) // 2)
            level(B_LEVELS + 1)
            pe.wait_ge(level_kept, B_LEVELS + 2)
            pe.wait_ge(bv_copied, 4)
            for h in range(TT):
                for d in range(B_HEADS):
                    o = psum[:, 2 * h + d // 2, (d % 2) * B_HV:(d % 2 + 1) * B_HV]
                    if h == 1:
                        product(o, score_x[:, d, :], bv[:, 0, d * B_HV:(d + 1) * B_HV], start=True)
                    ins = product(o, score_in[:, TT * d + h, :], bv[:, h, d * B_HV:(d + 1) * B_HV], start=h == 0, stop=True)
                ins.then_inc(o_done, 1)
            for h in range(TT):
                for half in range(2):
                    pe.wait_ge(o_ready, B_HEADS * h + 2 * half + 2)
                    turn(bo[:, h, half * BANK:(half + 1) * BANK], 4 + 2 * h + half, KB // 2).then_inc(o_turned, 1)
            pe.wait_ge(oT_hi_ready, 2 * TT - 1)
            for kb in range(KB):
                n = BOUT + kb
                if kb == KB // 2:
                    pe.wait_ge(oT_hi_ready, 2 * TT)
                moving_tile(n % 2, n + 1, lo_count(n), 0, hT_hi[:, kb, :], hT_lo[:, kb, :], kb == 0, kb == KB - 1,
                            (oT_lo_ready, 2 * TT) if kb == 0 else None, half=half_done[3] if kb == KB - 1 else None)
            peer(1)


def _layout(i):
    a = {k: np.asarray(v) for k, v in i.items()}

    def moving(w, blocks):
        kb = w.shape[0] // P
        return w.reshape(kb, P, blocks, TILE).transpose(2, 0, 1, 3).reshape(blocks * kb, P, TILE)

    def stationary(w):
        n = w.shape[1] // P
        return w.reshape(KB, P, n, P).transpose(2, 1, 0, 3).reshape(n, P, TILE)

    s, tk = np.arange(P)[:, None], np.arange(P)[None, :]
    masks = [((s ^ tk) >> j == 1) & (tk > s) for j in range(B_LEVELS)] + [s == tk]
    b_w = a["b_w_in"][0]
    v_first = np.concatenate([a["a_w_in"][0][:, A_WIDTH:], a["a_w_in"][0][:, :A_WIDTH]], axis=1)
    r = {
        "x": a["x"][0],
        "a_in": moving(v_first, A_BLOCKS),
        "a_out": moving(a["a_w_out"][0], 1),
        "b_in": np.concatenate([a["a_b_in"][0][A_WIDTH:], a["a_b_in"][0][:A_WIDTH]]),
        "ln_g": a["a_ln_g"][0],
        "ln_b": a["a_ln_b"][0],
        "w_sT": a["a_w_s"][0].transpose(2, 0, 1),
        "b_sT": a["a_b_s"][0].T,
        "gains": np.stack([a[k][l] for l in range(2) for k in ("norm_mix", "norm_ffn")] + [a["final_norm"]]),
        "keysT": np.stack([np.stack([a[k][l].T for k in ("p_k1", "p_k2")], axis=1) for l in range(2)], axis=1),
        "b_qk": stationary(b_w[:, :2 * B_KEY]),
        "b_rv": moving(np.concatenate([b_w[:, 2 * B_KEY + D:2 * B_KEY + 2 * D], b_w[:, 2 * B_KEY:2 * B_KEY + D]], axis=1), 2),
        "w_g": b_w[:, 2 * B_KEY + 2 * D:].reshape(KB, P, B_RANK).transpose(1, 0, 2),
        "w_g2": a["b_w_g2"][0],
        "b_g": a["b_b_g"][0],
        "b_norm": a["b_norm"][0],
        "b_out": moving(a["b_w_out"][0], 1),
        "consts": np.stack([np.eye(P), np.broadcast_to(np.arange(P), (P, P)), (s <= tk) / 16.0], axis=1).astype(np.float32),
        "masks": np.stack(masks, axis=1).astype(np.uint32),
    }
    for l in range(2):
        r[f"w_q{l}"] = stationary(a["p_w_q"][l])
        r[f"u{l}"] = a["p_u"][l].reshape(NK, NK, KB, P).transpose(1, 3, 2, 0).reshape(NK, P, TILE)
        r[f"v{l}"] = a["p_v"][l].reshape(NK, NK, D).transpose(1, 0, 2)
    return {k: np.ascontiguousarray(v) for k, v in r.items()}


def kernel(**inputs):
    import concourse.bacc as bacc
    from concourse.bass_utils import run_bass_kernel_spmd

    arrays = _layout(inputs)
    nc = bacc.Bacc("TRN2", target_bir_lowering=False, num_devices=1)
    t = {k: nc.dram_tensor(f"in_{k}", v.shape, mybir.dt.from_np(v.dtype), kind="ExternalInput").ap() for k, v in arrays.items()}
    out = nc.dram_tensor("out_0", (TT, P, D), F32, kind="ExternalOutput").ap()
    trunk(nc, t, out)
    r = run_bass_kernel_spmd(nc, [{f"in_{k}": v for k, v in arrays.items()}], core_ids=[0])
    return r.results[0]["out_0"].reshape(1, T, D)
```
